# Optimizing a Trainium2 kernel written in Bass

```python
import math
import jax, jax.numpy as jnp
from jax import lax
import numpy as np

D_MODEL = 1024
BATCH = 1
SEQ = 256
DEPTH = 1

D_MIX = D_MODEL
D_MLSTM = D_MIX // 2
D_DIFF = D_MIX - D_MLSTM
ML_HEADS = 4
ML_HD = D_MLSTM // ML_HEADS
CONV_W = 4
CHUNK = 128
DA_HEADS = 4
DA_VD = D_DIFF // DA_HEADS
DA_QD = DA_VD // 2
Q_BLOCK = 128
REL_BUCKETS = 32
REL_MAX_DIST = 128
N_GROUPS = 4
EXP_PER_GROUP = 8
N_EXPERTS = N_GROUPS * EXP_PER_GROUP
TOP_K_FINE = 2
D_FF_EXP = 512
EPS = 1e-6
SUBLN_EPS = 1e-5
IN_COLS = 3 * D_MLSTM + 3 * D_DIFF


def rmsnorm(x, g, eps=EPS):
    xf = x.astype(jnp.float32)
    y = xf * lax.rsqrt(jnp.mean(xf * xf, axis=-1, keepdims=True) + eps)
    return (y * g.astype(jnp.float32)).astype(x.dtype)

def head_layernorm(h, g):
    mu = jnp.mean(h, axis=-1, keepdims=True)
    var = jnp.mean(jnp.square(h - mu), axis=-1, keepdims=True)
    return (h - mu) * lax.rsqrt(var + EPS) * g.astype(jnp.float32)

def causal_conv(x, w, b):
    c = x.shape[-1]
    y = lax.conv_general_dilated(x, w[:, None, :].astype(x.dtype), window_strides=(1,),
                                 padding=[(CONV_W - 1, 0)],
                                 dimension_numbers=('NWC', 'WIO', 'NWC'),
                                 feature_group_count=c)
    return y + b.astype(x.dtype)

def mlstm_chunkwise(q, k, v, i_pre, logf):
    bsz, s, nh, d = q.shape
    nc = s // CHUNK
    def chunks(t):
        return t.reshape(bsz, nc, CHUNK, nh, d).transpose(1, 0, 3, 2, 4)
    def gchunks(t):
        return t.reshape(bsz, nc, CHUNK, nh).transpose(1, 0, 3, 2)
    tril = jnp.tril(jnp.ones((CHUNK, CHUNK), dtype=bool))

    def step(carry, xs):
        cmat, nvec, m = carry
        qc, kc, vc, ic, fc = xs
        b = jnp.cumsum(fc, axis=-1)
        inter = b + m[..., None]
        dmat = jnp.where(tril, b[..., :, None] - b[..., None, :] + ic[..., None, :], -jnp.inf)
        m_t = jnp.maximum(inter, jnp.max(dmat, axis=-1))
        w = jnp.exp(dmat - m_t[..., None]) * jnp.einsum('bhtd,bhsd->bhts', qc, kc)
        sp = jnp.exp(inter - m_t)
        num = sp[..., None] * jnp.einsum('bhtk,bhvk->bhtv', qc, cmat) + jnp.einsum('bhts,bhsv->bhtv', w, vc)
        den = sp * jnp.einsum('bhtk,bhk->bht', qc, nvec) + jnp.sum(w, axis=-1)
        h = num / jnp.maximum(jnp.abs(den), jnp.exp(-m_t))[..., None]
        b_end = b[..., -1]
        g = b_end[..., None] - b + ic
        m_new = jnp.maximum(b_end + m, jnp.max(g, axis=-1))
        wk = jnp.exp(g - m_new[..., None])
        decay = jnp.exp(b_end + m - m_new)
        c_new = decay[..., None, None] * cmat + jnp.einsum('bhs,bhsv,bhsk->bhvk', wk, vc, kc)
        n_new = decay[..., None] * nvec + jnp.einsum('bhs,bhsk->bhk', wk, kc)
        return (c_new, n_new, m_new), h

    init = (jnp.zeros((bsz, nh, d, d), jnp.float32), jnp.zeros((bsz, nh, d), jnp.float32),
            jnp.zeros((bsz, nh), jnp.float32))
    _, hs = lax.scan(step, init, (chunks(q), chunks(k), chunks(v), gchunks(i_pre), gchunks(logf)))
    return hs.transpose(1, 0, 3, 2, 4).reshape(bsz, s, nh, d)

def mlstm_group(c, v, z, conv_w, conv_b, w_mq, w_mk, w_mgate, b_mgate, m_norm_g, m_skip):
    bsz, s, _ = c.shape
    c_act = jax.nn.silu(causal_conv(c, conv_w, conv_b))
    ch = c_act.reshape(bsz, s, ML_HEADS, ML_HD)
    q = jnp.einsum('bshd,hde->bshe', ch, w_mq)
    k = jnp.einsum('bshd,hde->bshe', ch, w_mk)
    vh = v.reshape(bsz, s, ML_HEADS, ML_HD)
    gin = jnp.concatenate([q.reshape(bsz, s, -1), k.reshape(bsz, s, -1), v], axis=-1)
    gates = (gin @ w_mgate).astype(jnp.float32) + b_mgate.astype(jnp.float32)
    i_pre = gates[..., :ML_HEADS]
    logf = jax.nn.log_sigmoid(gates[..., ML_HEADS:])
    h = mlstm_chunkwise(q.astype(jnp.float32), (k * (ML_HD ** -0.5)).astype(jnp.float32),
                        vh.astype(jnp.float32), i_pre, logf)
    h = head_layernorm(h, m_norm_g.reshape(ML_HEADS, ML_HD)).reshape(bsz, s, D_MLSTM)
    h = h + m_skip.astype(jnp.float32) * c_act.astype(jnp.float32)
    o = jax.nn.sigmoid(z.astype(jnp.float32))
    return (o * h).astype(c.dtype)

def rel_bucket(qpos, kpos):
    n = jnp.maximum(qpos[:, None] - kpos[None, :], 0)
    max_exact = REL_BUCKETS // 2
    large = max_exact + (jnp.log(jnp.maximum(n, 1).astype(jnp.float32) / max_exact)
                         / math.log(REL_MAX_DIST / max_exact) * (REL_BUCKETS - max_exact)).astype(jnp.int32)
    large = jnp.minimum(large, REL_BUCKETS - 1)
    return jnp.where(n < max_exact, n, large)

def diff_attention(q, k, v, lam, rel_bias):
    bsz, s = q.shape[0], q.shape[1]
    nb = s // Q_BLOCK
    scale = DA_QD ** -0.5
    qb = jnp.moveaxis(q.reshape(bsz, nb, Q_BLOCK, DA_HEADS, 2, DA_QD), 1, 0)
    kpos = jnp.arange(s)

    def block(args):
        q_blk, bi = args
        qpos = bi * Q_BLOCK + jnp.arange(Q_BLOCK)
        bias = rel_bias[rel_bucket(qpos, kpos)].transpose(2, 0, 1).astype(jnp.float32)
        mask = kpos[None, :] <= qpos[:, None]
        logits = jnp.einsum('bqhcd,bkhcd->bchqk', q_blk, k).astype(jnp.float32) * scale + bias[None, None]
        p = jax.nn.softmax(jnp.where(mask, logits, -jnp.inf), axis=-1)
        a = p[:, 0] - lam * p[:, 1]
        return jnp.einsum('bhqk,bkhd->bqhd', a.astype(v.dtype), v)

    out = lax.map(block, (qb, jnp.arange(nb)))
    return jnp.moveaxis(out, 0, 1).reshape(bsz, s, DA_HEADS, DA_VD)

def hier_moe(h, w_rg, b_rg, w_re, b_re, w_eg, w_eu, w_ed):
    bsz, s, d = h.shape
    t = h.reshape(-1, d)
    lg = (t @ w_rg).astype(jnp.float32) + b_rg.astype(jnp.float32)
    pg = jax.nn.softmax(lg, axis=-1)
    _, g_idx = lax.top_k(lg, 1)
    pg_sel = jnp.take_along_axis(pg, g_idx, axis=-1)
    le = jnp.einsum('nd,dge->nge', t, w_re).astype(jnp.float32) + b_re.astype(jnp.float32)
    le_sel = jnp.take_along_axis(le, g_idx[:, :, None], axis=1)[:, 0]
    top_v, top_i = lax.top_k(le_sel, TOP_K_FINE)
    pw = jax.nn.softmax(top_v, axis=-1)
    eid = g_idx * EXP_PER_GROUP + top_i
    gates = jnp.sum(jax.nn.one_hot(eid, N_EXPERTS, dtype=jnp.float32) * (pg_sel * pw)[..., None], axis=1)
    gates = gates.astype(t.dtype)
    out = jnp.zeros_like(t)
    for e in range(N_EXPERTS):
        hid = jax.nn.silu(t @ w_eg[e]) * (t @ w_eu[e])
        out = out + gates[:, e:e + 1] * (hid @ w_ed[e])
    return out.reshape(bsz, s, d)

def first_inputs(seed: int = 0) -> dict:
    key = jax.random.key(seed)
    ks = jax.random.split(key, 32)
    f32 = jnp.float32
    def nrm(k, shape, sc):
        return jax.random.normal(k, shape, f32) * sc
    L = DEPTH
    b_i = nrm(ks[7], (L, ML_HEADS), 0.1)
    b_f = jnp.linspace(3.0, 6.0, ML_HEADS, dtype=f32)[None, :] + nrm(ks[8], (L, ML_HEADS), 0.01)
    return {
        'x': nrm(ks[0], (BATCH, SEQ, D_MODEL), 1.0),
        'w_in': nrm(ks[1], (L, D_MODEL, IN_COLS), D_MODEL ** -0.5),
        'conv_w': nrm(ks[2], (L, CONV_W, D_MLSTM), CONV_W ** -0.5),
        'conv_b': nrm(ks[3], (L, D_MLSTM), 0.01),
        'w_mq': nrm(ks[4], (L, ML_HEADS, ML_HD, ML_HD), ML_HD ** -0.5),
        'w_mk': nrm(ks[5], (L, ML_HEADS, ML_HD, ML_HD), ML_HD ** -0.5),
        'w_mgate': nrm(ks[6], (L, 3 * D_MLSTM, 2 * ML_HEADS), 0.1 * (3 * D_MLSTM) ** -0.5),
        'b_mgate': jnp.concatenate([b_i, b_f], axis=-1),
        'm_norm_g': 1.0 + nrm(ks[9], (L, D_MLSTM), 0.02),
        'm_skip': 1.0 + nrm(ks[10], (L, D_MLSTM), 0.02),
        'lambda_qk': nrm(ks[11], (L, 4, DA_QD), 0.1),
        'da_norm_g': 1.0 + nrm(ks[12], (L, DA_VD), 0.02),
        'rel_bias': nrm(ks[13], (REL_BUCKETS, DA_HEADS), 0.2),
        'w_out': nrm(ks[14], (L, D_MIX, D_MODEL), D_MIX ** -0.5),
        'norm1_g': 1.0 + nrm(ks[15], (L, D_MODEL), 0.02),
        'norm2_g': 1.0 + nrm(ks[16], (L, D_MODEL), 0.02),
        'w_rg': nrm(ks[17], (L, D_MODEL, N_GROUPS), D_MODEL ** -0.5),
        'b_rg': nrm(ks[18], (L, N_GROUPS), 0.01),
        'w_re': nrm(ks[19], (L, D_MODEL, N_GROUPS, EXP_PER_GROUP), D_MODEL ** -0.5),
        'b_re': nrm(ks[20], (L, N_GROUPS, EXP_PER_GROUP), 0.01),
        'w_eg': nrm(ks[21], (L, N_EXPERTS, D_MODEL, D_FF_EXP), D_MODEL ** -0.5),
        'w_eu': nrm(ks[22], (L, N_EXPERTS, D_MODEL, D_FF_EXP), D_MODEL ** -0.5),
        'w_ed': nrm(ks[23], (L, N_EXPERTS, D_FF_EXP, D_MODEL), D_FF_EXP ** -0.5),
        'normf_g': 1.0 + nrm(ks[24], (D_MODEL,), 0.02),
    }

def first_block(x, w_in, conv_w, conv_b, w_mq, w_mk, w_mgate, b_mgate, m_norm_g, m_skip,
              lambda_qk, da_norm_g, rel_bias, w_out, norm1_g, norm2_g, w_rg, b_rg, w_re, b_re,
              w_eg, w_eu, w_ed, normf_g):
    bsz, s, _ = x.shape
    splits = [D_MLSTM, 2 * D_MLSTM, 3 * D_MLSTM, 3 * D_MLSTM + D_DIFF, 3 * D_MLSTM + 2 * D_DIFF]
    for l in range(DEPTH):
        lam_init = 0.8 - 0.6 * math.exp(-0.3 * l)
        h = rmsnorm(x, norm1_g[l])
        proj = h @ w_in[l]
        c, vm, z, qd, kd, vd = jnp.split(proj, splits, axis=-1)
        y_m = mlstm_group(c, vm, z, conv_w[l], conv_b[l], w_mq[l], w_mk[l], w_mgate[l], b_mgate[l],
                          m_norm_g[l], m_skip[l])
        lq = lambda_qk[l].astype(jnp.float32)
        lam = jnp.exp(jnp.dot(lq[0], lq[1])) - jnp.exp(jnp.dot(lq[2], lq[3])) + lam_init
        y_d = diff_attention(qd.reshape(bsz, s, DA_HEADS, 2, DA_QD), kd.reshape(bsz, s, DA_HEADS, 2, DA_QD),
                             vd.reshape(bsz, s, DA_HEADS, DA_VD), lam, rel_bias)
        y_d = (rmsnorm(y_d, da_norm_g[l], SUBLN_EPS) * (1.0 - lam_init)).reshape(bsz, s, D_DIFF)
        x = x + jnp.concatenate([y_m, y_d.astype(x.dtype)], axis=-1) @ w_out[l]
        h2 = rmsnorm(x, norm2_g[l])
        x = x + hier_moe(h2, w_rg[l], b_rg[l], w_re[l], b_re[l], w_eg[l], w_eu[l], w_ed[l])
    return rmsnorm(x, normf_g)


DEPTH_2 = 2

PLE_DIM = 256
D_FF = 2816
ROPE_THETA = 10000.0
RET_THETA = 10000.0
N_NORMS = 7

A_HEADS = 4
A_DK = 128
A_DV = 128
A_CHUNK = 64
B_Q_HEADS = 8
B_KV_HEADS = 2
B_HEAD_DIM = 64
B_WINDOW = 128
B_BLOCK = 128
C_HEADS = 4
C_DK = 256
C_DV = 512
C_CHUNK = 128

N_EVEN = (DEPTH_2 + 1) // 2
N_ODD = DEPTH_2 // 2

A_KW = A_HEADS * A_DK
A_VW = A_HEADS * A_DV
B_QW = B_Q_HEADS * B_HEAD_DIM
B_KW = B_KV_HEADS * B_HEAD_DIM
EVEN_SPLITS = [A_KW, 2 * A_KW, 2 * A_KW + A_VW, 2 * A_KW + 2 * A_VW, 2 * A_KW + 2 * A_VW + B_QW,
               2 * A_KW + 2 * A_VW + B_QW + B_KW]
EVEN_IN = 2 * A_KW + 2 * A_VW + B_QW + 2 * B_KW
EVEN_OUT = A_VW + B_QW
C_KW = C_HEADS * C_DK
C_VW = C_HEADS * C_DV
ODD_SPLITS = [C_KW, 2 * C_KW, 2 * C_KW + C_VW]
ODD_IN = 2 * C_KW + 2 * C_VW
ODD_OUT = C_VW


def rmsnorm_2(x, g):
    xf = x.astype(jnp.float32)
    y = xf * lax.rsqrt(jnp.mean(xf * xf, axis=-1, keepdims=True) + EPS)
    return (y * g.astype(jnp.float32)).astype(x.dtype)

def swiglu(x, w_in, w_out):
    gate, up = jnp.split(x @ w_in, 2, axis=-1)
    return (jax.nn.silu(gate) * up) @ w_out

def rope_tables(positions, inv_freq):
    ang = positions.astype(jnp.float32)[:, :, None] * inv_freq[None, None, :]
    return jnp.cos(ang)[:, :, None, :], jnp.sin(ang)[:, :, None, :]

def apply_rope(x, cos, sin):
    xf = x.astype(jnp.float32)
    x1, x2 = jnp.split(xf, 2, axis=-1)
    return jnp.concatenate([x1 * cos - x2 * sin, x2 * cos + x1 * sin], axis=-1).astype(x.dtype)

def hgrn2_chunkwise(q, f_logit, i, lb):
    B, S, H, K = q.shape
    V = i.shape[-1]
    C = A_CHUNK
    n = S // C

    def chunks(t):
        return t.astype(jnp.float32).reshape(B, n, C, H, -1).transpose(0, 3, 1, 2, 4)

    lb5 = lb[None, :, None, None, :]
    qf = jax.nn.silu(chunks(q))
    f = lb5 + (1.0 - lb5) * jax.nn.sigmoid(chunks(f_logit))
    k = 1.0 - f
    v = chunks(i)
    b = jnp.cumsum(jnp.log(f), axis=3)
    b_last = b[:, :, :, -1:, :]
    q_s = qf * jnp.exp(b)
    k_s = k * jnp.exp(-b)
    k_d = k * jnp.exp(b_last - b)
    causal = jnp.tril(jnp.ones((C, C), dtype=bool))
    att = jnp.where(causal, jnp.einsum('bhnck,bhnsk->bhncs', q_s, k_s), 0.0)
    intra = jnp.einsum('bhncs,bhnsv->bhncv', att, v)
    dec = jnp.exp(b_last[:, :, :, 0, :])

    def step(state, xs):
        qc, kc, vc, dc = xs
        o = jnp.einsum('bhck,bhkv->bhcv', qc, state)
        state = state * dc[..., None] + jnp.einsum('bhck,bhcv->bhkv', kc, vc)
        return state, o

    xs = (jnp.moveaxis(q_s, 2, 0), jnp.moveaxis(k_d, 2, 0), jnp.moveaxis(v, 2, 0), jnp.moveaxis(dec, 2, 0))
    _, inter = lax.scan(step, jnp.zeros((B, H, K, V), jnp.float32), xs)
    o = intra + jnp.moveaxis(inter, 0, 2)
    return o.transpose(0, 2, 3, 1, 4).reshape(B, S, H, V)

def swa_with_sinks(q, k, v, sinks):
    B, S, Hq, D = q.shape
    G = k.shape[2]
    R = Hq // G
    L = B_BLOCK
    nb = S // L
    qb = q.reshape(B, nb, L, G, R, D)
    kb = k.reshape(B, nb, L, G, D)
    vb = v.reshape(B, nb, L, G, D)
    pad = ((0, 0), (1, 0), (0, 0), (0, 0), (0, 0))
    kk = jnp.concatenate([jnp.pad(kb[:, :-1], pad), kb], axis=2)
    vv = jnp.concatenate([jnp.pad(vb[:, :-1], pad), vb], axis=2)
    s = jnp.einsum('bnqgrd,bnkgd->bngrqk', qb, kk).astype(jnp.float32) * (D ** -0.5)
    qi = jnp.arange(L)[:, None]
    kj = jnp.arange(2 * L)[None, :]
    diff = qi + L - kj
    band = (diff >= 0) & (diff < B_WINDOW)
    key_pos = jnp.arange(nb)[:, None, None] * L - L + kj[None]
    valid = band[None] & (key_pos >= 0)
    s = jnp.where(valid[None, :, None, None], s, -jnp.inf)
    sink = sinks.astype(jnp.float32).reshape(G, R)[None, None, :, :, None, None]
    m = jnp.maximum(jnp.max(s, axis=-1, keepdims=True), sink)
    pr = jnp.exp(s - m)
    denom = jnp.sum(pr, axis=-1, keepdims=True) + jnp.exp(sink - m)
    o = jnp.einsum('bngrqk,bnkgd->bnqgrd', (pr / denom).astype(vv.dtype), vv)
    return o.reshape(B, S, Hq * D)

def retention_chunkwise(q, k, v):
    B, S, H, K = q.shape
    V = v.shape[-1]
    C = C_CHUNK
    n = S // C
    lg = jnp.log1p(-jnp.exp2(-5.0 - jnp.arange(H, dtype=jnp.float32)))

    def chunks(t):
        return t.astype(jnp.float32).reshape(B, n, C, H, -1).transpose(0, 3, 1, 2, 4)

    qc = chunks(q)
    kc = chunks(k) * (K ** -0.5)
    vc = chunks(v)
    idx = jnp.arange(C, dtype=jnp.float32)
    diff = idx[:, None] - idx[None, :]
    decay = jnp.where(diff >= 0, jnp.exp(jnp.maximum(diff, 0.0)[None] * lg[:, None, None]), 0.0)
    att = jnp.einsum('bhnck,bhnsk->bhncs', qc, kc) * decay[None, :, None]
    intra = jnp.einsum('bhncs,bhnsv->bhncv', att, vc)
    q_in = qc * jnp.exp((idx + 1.0)[None, :] * lg[:, None])[None, :, None, :, None]
    k_in = kc * jnp.exp((C - 1.0 - idx)[None, :] * lg[:, None])[None, :, None, :, None]
    chunk_dec = jnp.exp(C * lg)[None, :, None, None]

    def step(state, xs):
        qx, kx, vx = xs
        o = jnp.einsum('bhck,bhkv->bhcv', qx, state)
        state = state * chunk_dec + jnp.einsum('bhck,bhcv->bhkv', kx, vx)
        return state, o

    xs = (jnp.moveaxis(q_in, 2, 0), jnp.moveaxis(k_in, 2, 0), jnp.moveaxis(vc, 2, 0))
    _, inter = lax.scan(step, jnp.zeros((B, H, K, V), jnp.float32), xs)
    o = intra + jnp.moveaxis(inter, 0, 2)
    return o.transpose(0, 2, 3, 1, 4).reshape(B, S, H, V)

def even_mixer(u, w_in, w_out, lb, onorm_g, sinks, cos_b, sin_b):
    B, S, _ = u.shape
    qa, fa, ia, ga, qb, kb, vb = jnp.split(u @ w_in, EVEN_SPLITS, axis=-1)
    oa = hgrn2_chunkwise(qa.reshape(B, S, A_HEADS, A_DK), fa.reshape(B, S, A_HEADS, A_DK),
                         ia.reshape(B, S, A_HEADS, A_DV), lb.reshape(A_HEADS, A_DK))
    oa = rmsnorm_2(oa, onorm_g) * jax.nn.silu(ga.reshape(B, S, A_HEADS, A_DV).astype(jnp.float32))
    oa = oa.reshape(B, S, A_VW).astype(u.dtype)
    qh = apply_rope(qb.reshape(B, S, B_Q_HEADS, B_HEAD_DIM), cos_b, sin_b)
    kh = apply_rope(kb.reshape(B, S, B_KV_HEADS, B_HEAD_DIM), cos_b, sin_b)
    ob = swa_with_sinks(qh, kh, vb.reshape(B, S, B_KV_HEADS, B_HEAD_DIM), sinks).astype(u.dtype)
    return jnp.concatenate([oa, ob], axis=-1) @ w_out

def odd_mixer(u, w_in, w_out, onorm_g, cos_c, sin_c):
    B, S, _ = u.shape
    qc, kc, vc, gc = jnp.split(u @ w_in, ODD_SPLITS, axis=-1)
    qh = apply_rope(qc.reshape(B, S, C_HEADS, C_DK), cos_c, sin_c)
    kh = apply_rope(kc.reshape(B, S, C_HEADS, C_DK), cos_c, sin_c)
    o = retention_chunkwise(qh, kh, vc.reshape(B, S, C_HEADS, C_DV))
    o = rmsnorm_2(o, onorm_g) * jax.nn.silu(gc.reshape(B, S, C_HEADS, C_DV).astype(jnp.float32))
    return o.reshape(B, S, C_VW).astype(u.dtype) @ w_out

def second_inputs(seed: int = 0) -> dict:
    key = jax.random.key(seed)
    ks = jax.random.split(key, 18)
    f32 = jnp.float32

    def w(k, shape, fan_in):
        return jax.random.normal(k, shape, f32) * (fan_in ** -0.5)

    x = jax.random.normal(ks[0], (BATCH, SEQ, D_MODEL), f32)
    p = jax.random.normal(ks[1], (DEPTH_2, BATCH, SEQ, PLE_DIM), f32)
    offsets = jax.random.randint(ks[2], (BATCH, 1), 0, 4096, dtype=jnp.int32)
    positions = (offsets + jnp.arange(SEQ, dtype=jnp.int32)[None, :]).astype(jnp.int32)
    norm_g = 1.0 + 0.05 * jax.random.normal(ks[3], (DEPTH_2, N_NORMS, D_MODEL), f32)
    ffn1_w_in = w(ks[4], (DEPTH_2, D_MODEL, 2 * D_FF), D_MODEL)
    ffn1_w_out = w(ks[5], (DEPTH_2, D_FF, D_MODEL), D_FF)
    ffn2_w_in = w(ks[6], (DEPTH_2, D_MODEL, 2 * D_FF), D_MODEL)
    ffn2_w_out = w(ks[7], (DEPTH_2, D_FF, D_MODEL), D_FF)
    ple_w_proj = w(ks[8], (DEPTH_2, PLE_DIM, D_MODEL), PLE_DIM)
    ple_w_gate = w(ks[9], (DEPTH_2, D_MODEL, D_MODEL), D_MODEL)
    even_w_in = w(ks[10], (N_EVEN, D_MODEL, EVEN_IN), D_MODEL)
    even_w_out = w(ks[11], (N_EVEN, EVEN_OUT, D_MODEL), EVEN_OUT)
    hgrn_lb = 0.1 * jax.random.normal(ks[12], (N_EVEN + 1, A_KW), f32)
    hgrn_onorm_g = 1.0 + 0.05 * jax.random.normal(ks[13], (N_EVEN, A_DV), f32)
    attn_sinks = jax.random.normal(ks[14], (N_EVEN, B_Q_HEADS), f32)
    odd_w_in = w(ks[15], (N_ODD, D_MODEL, ODD_IN), D_MODEL)
    odd_w_out = w(ks[16], (N_ODD, ODD_OUT, D_MODEL), ODD_OUT)
    ret_onorm_g = 1.0 + 0.05 * jax.random.normal(ks[17], (N_ODD, C_DV), f32)
    return {'x': x, 'p': p, 'positions': positions, 'norm_g': norm_g,
            'ffn1_w_in': ffn1_w_in, 'ffn1_w_out': ffn1_w_out, 'ffn2_w_in': ffn2_w_in, 'ffn2_w_out': ffn2_w_out,
            'ple_w_proj': ple_w_proj, 'ple_w_gate': ple_w_gate,
            'even_w_in': even_w_in, 'even_w_out': even_w_out, 'hgrn_lb': hgrn_lb, 'hgrn_onorm_g': hgrn_onorm_g,
            'attn_sinks': attn_sinks, 'odd_w_in': odd_w_in, 'odd_w_out': odd_w_out, 'ret_onorm_g': ret_onorm_g}

def second_block(x, p, positions, norm_g, ffn1_w_in, ffn1_w_out, ffn2_w_in, ffn2_w_out, ple_w_proj, ple_w_gate,
              even_w_in, even_w_out, hgrn_lb, hgrn_onorm_g, attn_sinks, odd_w_in, odd_w_out, ret_onorm_g):
    inv_b = ROPE_THETA ** (-jnp.arange(0, B_HEAD_DIM, 2, dtype=jnp.float32) / B_HEAD_DIM)
    inv_c = RET_THETA ** (-jnp.linspace(0.0, 1.0, C_DK // 2, dtype=jnp.float32))
    cos_b, sin_b = rope_tables(positions, inv_b)
    cos_c, sin_c = rope_tables(positions, inv_c)
    lb_all = jnp.cumsum(jax.nn.softmax(hgrn_lb.astype(jnp.float32), axis=0), axis=0)
    h = x
    for i in range(DEPTH_2):
        g = norm_g[i]
        h = h + 0.5 * rmsnorm_2(swiglu(rmsnorm_2(h, g[0]), ffn1_w_in[i], ffn1_w_out[i]), g[1])
        u = rmsnorm_2(h, g[2])
        j = i // 2
        if i % 2 == 0:
            mix = even_mixer(u, even_w_in[j], even_w_out[j], lb_all[j], hgrn_onorm_g[j], attn_sinks[j], cos_b, sin_b)
        else:
            mix = odd_mixer(u, odd_w_in[j], odd_w_out[j], ret_onorm_g[j], cos_c, sin_c)
        h = h + rmsnorm_2(mix, g[3])
        h = h + 0.5 * rmsnorm_2(swiglu(rmsnorm_2(h, g[4]), ffn2_w_in[i], ffn2_w_out[i]), g[5])
        gate = jax.nn.sigmoid(h @ ple_w_gate[i])
        h = h + rmsnorm_2(gate * (p[i] @ ple_w_proj[i]), g[6])
    return h


def setup_inputs(seed=0):
    out = dict(first_inputs(seed))
    for name, value in second_inputs(seed + 1).items():
        if name != "x":
            out[name + "_2"] = value
    return out


def reference(
    x, w_in, conv_w, conv_b, w_mq, w_mk, w_mgate, b_mgate, m_norm_g, m_skip, lambda_qk,
    da_norm_g, rel_bias, w_out, norm1_g, norm2_g, w_rg, b_rg, w_re, b_re, w_eg, w_eu, w_ed,
    normf_g, p_2, positions_2, norm_g_2, ffn1_w_in_2, ffn1_w_out_2, ffn2_w_in_2, ffn2_w_out_2,
    ple_w_proj_2, ple_w_gate_2, even_w_in_2, even_w_out_2, hgrn_lb_2, hgrn_onorm_g_2,
    attn_sinks_2, odd_w_in_2, odd_w_out_2, ret_onorm_g_2,
):
    x = first_block(
        x, w_in, conv_w, conv_b, w_mq, w_mk, w_mgate, b_mgate, m_norm_g, m_skip, lambda_qk,
        da_norm_g, rel_bias, w_out, norm1_g, norm2_g, w_rg, b_rg, w_re, b_re, w_eg, w_eu, w_ed,
        normf_g,
    )
    return second_block(
        x, p_2, positions_2, norm_g_2, ffn1_w_in_2, ffn1_w_out_2, ffn2_w_in_2, ffn2_w_out_2,
        ple_w_proj_2, ple_w_gate_2, even_w_in_2, even_w_out_2, hgrn_lb_2, hgrn_onorm_g_2,
        attn_sinks_2, odd_w_in_2, odd_w_out_2, ret_onorm_g_2,
    )


_drawn_inputs = setup_inputs


def setup_inputs(seed=0):
    import zlib

    import numpy as np

    out = dict(_drawn_inputs(seed))
    spreads = {}
    factors = {'b_rg': 3.401,
     'b_re': 3.521,
     'hgrn_lb_2': 6.872,
     'conv_b': 5.058,
     'm_norm_g': 3.312,
     'm_skip': 12.664,
     'da_norm_g': 2.976,
     'norm2_g': 2.815}
    for name, (base, spread) in spreads.items():
        noise = np.random.default_rng([zlib.crc32(name.encode()), seed]).standard_normal(out[name].shape)
        drawn = base * np.exp(spread * noise) if base else spread * noise
        out[name] = __import__('jax').numpy.asarray(drawn.astype(out[name].dtype))
    for name, factor in factors.items():
        out[name] = (out[name] * factor).astype(out[name].dtype)
    return out
```

```python
from contextlib import ExitStack

import numpy as np
import concourse.bass as bass
from concourse import mybir

ALU = mybir.AluOpType
ACT = mybir.ActivationFunctionType
F32 = mybir.dt.float32
F32R = mybir.dt.float32r
I32 = mybir.dt.int32
AX = mybir.AxisListType.X

P = 128
T = 256
NT = T // P
D = 1024
KC = D // P
UNIT = 2048
RING = 6
NH = 4
FF = 2816
FB = FF // 256
E = 32
CAP = 64
ROUNDS = T // CAP
BIG = 1.0e6
NEG = -1.0e30
EPS = 1e-6
SUBLN_EPS = 1e-5
LAM0 = 0.8 - 0.6
TWO_PI = 6.283185307179586

COLS = {}


def _table(entries):
    parts, at = [], 0
    for name, a in entries:
        a = np.asarray(a, np.float32)
        full = np.zeros((P, a.shape[1]), np.float32)
        full[:a.shape[0]] = a
        COLS[name] = (at, a.shape[1])
        at += a.shape[1]
        parts.append(full)
    return np.concatenate(parts, axis=1)


def _tables():
    i = np.arange(P)
    j = np.arange(2 * P)
    upto = (i[:, None] <= i[None, :]).astype(np.float32)
    always = _table([
        ("ident", np.eye(P)),
        ("fold", np.concatenate([np.eye(CAP), np.eye(CAP)])),
        ("mask3", np.concatenate([upto, np.ones((P, P)), upto], axis=1)),
        ("before", (i[:, None] < i[None, :])),
        ("slot", np.tile(np.arange(CAP) - BIG, 2)[None, :] * np.ones((P, 1))),
        ("tie", np.concatenate([4 - np.arange(4), 8 - np.arange(8)])[None, :] * np.ones((P, 1))),
    ])
    m = np.arange(2 * T - 1 - P)
    n = np.maximum(T - 1 - m, 0)
    large = 16 + (np.log(np.maximum(n, 1).astype(np.float32) / 16) / np.float32(np.log(8.0)) * 16).astype(np.int32)
    buckets = np.zeros((33, 384), np.float32)
    buckets[np.where(n < 16, n, np.minimum(large, 31)), m] = 1.0
    buckets[32, m] = m > T - 1
    first = _table([(f"sel{h}", (np.arange(NH)[:, None] == h) * np.ones((1, P))) for h in range(NH)]
                   + [("buckets", buckets)])
    dist = i[:, None] + P - j[None, :]
    band = np.where((dist >= 0) & (dist < P), 0.0, NEG)
    rot = np.zeros((P, P), np.float32)
    for f in range(P):
        rot[f + 32 if f % 64 < 32 else f - 32, f] = -1.0 if f % 64 < 32 else 1.0
    dup = [(np.arange(P)[:, None] == 64 * g + i[None, :] % 64) for g in range(2)]
    second = _table([
        ("band3", np.concatenate([band[:, P:], band], axis=1)),
        ("rot", rot), ("dup0", dup[0]), ("dup1", dup[1]),
        ("duprot0", rot[:, i % 64]), ("duprot1", rot[:, 64 + i % 64]),
        ("freq_b", (10000.0 ** (-np.arange(0, 64, 2, dtype=np.float32) / np.float32(64)))[i % 32][:, None]),
        ("freq_c", (10000.0 ** (-np.linspace(0.0, 1.0, P, dtype=np.float32)))[:, None]),
    ])
    return always, first, second


def _decays():
    lg = np.log1p(-np.exp2(-5.0 - np.arange(NH, dtype=np.float32))).astype(np.float32)
    d = (np.arange(T)[None, :] - np.arange(P)[:, None]).astype(np.float32)
    out = np.where(d[None] >= 0, np.exp(np.maximum(d, 0.0)[None] * lg[:, None, None]), 0.0) / 16.0
    return np.ascontiguousarray(out.transpose(1, 0, 2).reshape(P, NH * T).astype(np.float32))


ALWAYS, FIRST, SECOND = _tables()
DECAYS = _decays()
ALWAYS_NAMES = ("ident", "fold", "mask3", "before", "slot", "tie")


def two_block_kernel(nc, a, out):
    x_in = a["x"].rearrange("b (t p) d -> p (b t) d", p=P)
    out_v = out.rearrange("b (t p) d -> p (b t) d", p=P)
    scratch_dram = nc.dram_tensor("bias_rows", (NH, P, 384), F32, kind="Internal").ap()

    ctx = ExitStack()
    with ctx:
        def sb(name, shape, dt=F32):
            return ctx.enter_context(nc.sbuf_tensor(name, shape, dt))

        signals = {}

        def sig(name):
            if name not in signals:
                signals[name] = ctx.enter_context(nc.semaphore(name))
            return signals[name]

        ring_at = (nc.sbuf_base + 31) // 32 * 32
        raw = sb("raw", [P, RING, UNIT])
        wl = nc.alloc_sbuf_tensor_at("wl", [P, RING, UNIT], F32R, offset=ring_at)
        wh = sb("wh", [P, RING, UNIT], F32R)
        ah = sb("ah", [P, 16, T], F32R)
        al = sb("al", [P, 16, T], F32R)
        x = sb("x", [P, NT, D])
        arena = sb("arena", [P, 12288])
        scr = sb("scr", [P, 2048])
        cA = sb("cA", [P, ALWAYS.shape[1]])
        cB = sb("cB", [P, SECOND.shape[1]])
        gb = sb("gb", [P, D])
        vrow = gb[:, 0:256]
        vcol = sb("vcol", [P, 256])
        sm = sb("sm", [P, 176])
        nrounds_i = sb("nrounds_i", [1, 8], I32)
        acc = ctx.enter_context(nc.psum_tensor("acc", [P, 4, 512], F32))
        pw = ctx.enter_context(nc.psum_tensor("pw", [P, 4, 512], F32))

        def cst(name):
            c0, n = COLS[name]
            if name in ALWAYS_NAMES:
                return cA[:, c0:c0 + n]
            return cB[:, c0:c0 + n]

        ident = cst("ident")
        rd = ah[:, :, :].bitcast(F32)
        pF = arena[:, 0:5120]
        F_C, F_V, F_Z, F_Q, F_K = 0, 1024, 2048, 3072, 4096
        vd = arena[:, 5120:6144].rearrange("p (t n) -> p t n", t=NT)
        cact = arena[:, 6144:7168]
        mqk = arena[:, 7168:8192]
        qm, km = arena[:, 8192:9216], arena[:, 9216:10240]
        vt1 = arena[:, 10240:11272].rearrange("p (t h d) -> p t h d", t=NT, h=NH)
        wg = arena[:, 11272:11368].rearrange("p (c g) -> p c g", g=8)
        a_row, nm_row, mx_row = (scr[0:NH, k * T:(k + 1) * T] for k in range(3))
        mw = [scr[:, 384 * k:384 * (k + 1)] for k in range(2)]
        ob = arena[:, F_V:F_V + 1024].rearrange("p (t h d) -> p t h d", t=NT, h=NH)
        ob2 = arena[:, F_C:F_C + 1024].rearrange("p (t h d) -> p t h d", t=NT, h=NH)
        dlog = [a_.rearrange("p (c j) -> p c j", c=2) for a_ in (scr[:, 0:768], arena[:, 8192:8960])]
        dmix, dmixT = scr[:, 768:1152], scr[:, 1152:1536]
        btile = gb[:, :].rearrange("p (h j) -> p h j", h=NH)

        gbias = sm[:, 0:2]
        lamq = sm[:, 2:6]
        relb = sm[:, 6:10]
        brow = arena[:, 11368:11752]
        gus = arena[:, 0:1024]
        ydh = ah[:, 12:16, :].rearrange("p c t -> p (c t)")
        ydl = al[:, 10:14, :].rearrange("p c t -> p (c t)")
        slot_gate = sm[:, 172:173]
        selg = arena[:, 2048:2304].rearrange("p (t s) -> p t s", t=NT)
        selT = al[:, 14, :]
        gate_all = arena[:, 2560:2820].rearrange("p (t e) -> p t e", t=NT)
        pos_all = arena[:, 2820:3080].rearrange("p (t e) -> p t e", t=NT)
        wr = arena[:, 3080:3368].rearrange("p (c g) -> p c g", g=36)
        br = arena[:, 3368:3404]
        rt = arena[:, 3404:4096]
        h2 = arena[:, 4096:6144].rearrange("p (t d) -> p t d", t=NT)
        h2T = arena[:, 6144:8192].rearrange("p (c t) -> p c t", c=KC)
        masks = rt[:, 264:328].rearrange("p (t e) -> p t e", t=NT)
        now = rt[:, 328:334]
        silu_s = arena[:, 8192:8448]
        hid_s = arena[:, 8448:8704]
        zr = ctx.enter_context(nc.sbuf_tensor("zr", [P, P], F32R))
        sel = ctx.enter_context(nc.sbuf_tensor("sel", [P, NT, CAP], F32R))
        h2h = ah[:, 0:8, :].rearrange("p c t -> p (c t)").rearrange("p (t k f) -> p t k f", t=NT, k=KC)
        h2l = al[:, 0:8, :].rearrange("p c t -> p (c t)").rearrange("p (t k f) -> p t k f", t=NT, k=KC)
        xg = ah[:, 8:12, :].rearrange("p c t -> p (c t)").rearrange("p (k s) -> p k s", k=KC)
        hid = al[:, 8:10, :].rearrange("p c t -> p (c t)").rearrange("p (c s) -> p c s", c=4)
        sinks = sm[:, 160:168]
        qs, fk, ga = arena[:, 0:1024], arena[:, 1024:2048], arena[:, 2048:3072]
        qb, kb = arena[:, 3072:4096], arena[:, 4096:4352]
        ia = arena[:, 4352:5376].rearrange("p (t n) -> p t n", t=NT)
        vb = arena[:, 5376:5632].rearrange("p (t n) -> p t n", t=NT)
        qr, kr = arena[:, 5632:6656], arena[:, 6656:7168]
        kd, bsum, eb, ks = (arena[:, 7680 + 1024 * k:8704 + 1024 * k] for k in range(4))
        oh = bsum.rearrange("p (t h d) -> p t h d", t=NT, h=NH)
        swl = [scr[:, 384 * k:384 * (k + 1)] for k in range(2)]
        swt = [scr[:, 768 + 384 * k:768 + 384 * (k + 1)] for k in range(2)]
        vo = arena[:, 4096:8192].rearrange("p (t n) -> p t n", t=NT)
        go = arena[:, 8192:12288]
        oo = arena[:, 0:4096].rearrange("p (g d) -> p g d", g=8)
        ratt = [scr[:, 512 + 384 * k:896 + 384 * k] for k in range(2)]
        rope = ((arena[:, 7168:7424], arena[:, 7680:7936], arena[:, 7168:7424], arena[:, 7424:7680]),
                (scr[:, 512:768], scr[:, 768:1024], scr[:, 0:256], scr[:, 256:512]))
        trig_in = (arena[:, 7936:8192], scr[:, 1024:1280])
        junk1 = arena[:, 8192:10240].rearrange("p (t d) -> p t d", t=NT)
        junk = arena[:, 4096:6144].rearrange("p (t d) -> p t d", t=NT)
        diag = arena[:, 6144:6400].rearrange("p (t n) -> p t n", t=NT)
        sg = arena[:, 0:2048].rearrange("p (t d) -> p t d", t=NT)
        pt = arena[:, 2048:2560].rearrange("p (t n) -> p t n", t=NT)

        def cols_unit(w, c0):
            return w[:, c0:c0 + 256].rearrange("(k p) n -> p k n", p=P)

        def rows_unit(w, k0):
            return w[k0 * P:(k0 + 2) * P, :].rearrange("(k p) n -> p k n", p=P)

        block = ctx.enter_context(nc.Block())
        NA = 16
        UB, n = {}, 0
        for l in range(2):
            for name, count in (("ffn1", 33), ("mix_in", 11 if l == 0 else 24), ("mix_out", 4 if l == 0 else 8),
                                ("ffn2", 33), ("ple_gate", 4), ("ple_proj", 1)):
                UB[(l, name)] = n
                n += count

        def norm_col(l, n, c):
            k = (l * 7 + n) * KC + c
            return vcol[:, k:k + 1]

        def small_col(k):
            return vcol[:, P + k:P + k + 1]
        V_CW, V_CB, V_MG, V_SK, V_DA, V_LB, V_HG, V_RG = 0, 16, 20, 24, 28, 29, 37, 38

        class Waits:
            def __init__(self, eng):
                self.eng, self.seen = eng, {}

            def more(self, name, n=1):
                self.seen[name] = self.seen.get(name, 0) + n
                self.eng.wait_ge(sig(name), self.seen[name])

            def passed(self, name, n=1):
                self.seen[name] = self.seen.get(name, 0) + n

        @block.sync
        def _(sp):
            w = Waits(sp)

            def load(ep, u, src, it=0, shape="p k n -> p (k n)"):
                sp.wait_ge(sig(f"{ep}_used"), it * RING + (u + 1))
                if not isinstance(it, int):
                    sp.wait_ge(sig("x_loaded"), 16)
                slot = u % RING
                k = src.shape[1]
                dst = raw[:, slot, :].rearrange("p (k n) -> p k n", k=k)
                sp.dma_start(dst[:, :, 0:src.shape[2]], src).then_inc(sig(f"{ep}_landed{slot}"), 16)

            w_in, w_out = a["w_in"][0], a["w_out"][0]
            sp.dma_start(x[:, :, :], x_in).then_inc(sig("x_loaded"), 16)
            for u in range(12):
                if u == 2:
                    sp.wait_ge(sig("rows"), 160)
                load("a", u, cols_unit(w_in, u * 256))
            for u in range(4):
                load("a", 12 + u, rows_unit(w_out, 2 * u))

            def expert(e, it):
                for j in range(4):
                    wt = a["w_eg"] if j < 2 else a["w_eu"]
                    src = wt[0, bass.ds(e, 1)].rearrange("o (p k) n -> p (o k) n", k=KC)[:, 4 * (j % 2):4 * (j % 2) + 4, :]
                    load("m", j, src, it)
                for j in range(2):
                    src = a["w_ed"][0, bass.ds(e, 1)].rearrange("o (k p) n -> p (o k) n", p=P)[:, 2 * j:2 * j + 2, :]
                    load("m", 4 + j, src, it)

            with sp.Fori(0, E) as e:
                expert(e, e)
            sp.wait_ge(sig("rounds_ready"), 1)
            nr = sp.value_load(nrounds_i[0:1, 0:1], min_val=0, max_val=ROUNDS - 1)
            with sp.If(nr > 0):
                with sp.Fori(0, nr) as r:
                    with sp.Fori(0, E) as e:
                        expert(e, (r + 1) * E + e)
            with sp.Else():
                sp.nop()
            w1 = a["ffn1_w_in_2"][0]
            load("m", 0, cols_unit(w1, 0), nr * E + E)
            load("m", 1, cols_unit(w1, FF), nr * E + E)

            def ffn(l, n):
                w1, w2, u0 = a[f"ffn{n}_w_in_2"][l], a[f"ffn{n}_w_out_2"][l], UB[(l, f"ffn{n}")]
                if u0 > 0:
                    load("b", u0, cols_unit(w1, 0))
                    load("b", u0 + 1, cols_unit(w1, FF))
                w1v = w1.rearrange("(k p) n -> p k n", p=P)
                w2v = w2.rearrange("(b k p) n -> p b k n", p=P, k=2)
                with sp.Fori(0, 5) as it:
                    for par in range(2):
                        u = u0 + 2 + 3 * par
                        load("b", u, w1v[:, :, bass.ds(it * 512 + (par + 1) * 256, 256)], it)
                        load("b", u + 1, w1v[:, :, bass.ds(it * 512 + (FF + (par + 1) * 256), 256)], it)
                        load("b", u + 2, w2v[:, bass.ds(it * 2 + par, 1)].rearrange("p o k n -> p (o k) n"), it)
                load("b", u0 + 32, rows_unit(w2, 20))

            for l in range(2):
                ffn(l, 1)
                if l == 0:
                    w1, w2 = a["even_w_in_2"][0], a["even_w_out_2"][0]
                else:
                    w1, w2 = a["odd_w_in_2"][0], a["odd_w_out_2"][0]
                for j in range(UB[(l, "mix_out")] - UB[(l, "mix_in")]):
                    load("b", UB[(l, "mix_in")] + j, cols_unit(w1, j * 256))
                for j in range(UB[(l, "ffn2")] - UB[(l, "mix_out")]):
                    load("b", UB[(l, "mix_out")] + j, rows_unit(w2, 2 * j if l else (2 * j + 4) % 8))
                ffn(l, 2)
                for j in range(4):
                    load("b", UB[(l, "ple_gate")] + j, rows_unit(a["ple_w_gate_2"][l], 2 * j))
                load("b", UB[(l, "ple_proj")], rows_unit(a["ple_w_proj_2"][l], 0))
            sp.wait_ge(sig("out_ready"), 1)
            sp.dma_start(out_v, x[:, :, :]).then_inc(sig("out_stored"), 16)
            sp.wait_ge(sig("out_stored"), 16)

        @block.gpsimd
        def _(pool):
            w = Waits(pool)

            def small(dst, src, name):
                pool.dma_start(dst, src, allow_slow_non_contiguous=True).then_inc(sig(name), 16)

            def gain(vec, offset):
                small(gb[:, :], bass.AP(vec.tensor, offset, [[0, P], [1, D]]), "gain_loaded")

            pool.memset(vrow, 0.0).then_inc(sig("rows_zero"), 1)
            w.more("rows_zero")
            small(cA[:, :], a["consts_always"], "consts")
            small(cB[:, 0:FIRST.shape[1]], a["consts_first"], "consts")
            small(vrow[0:112, 0:128], a["norm_g_2"].rearrange("l n (c p) -> (l n c) p", p=P), "rows")
            small(vrow[112:120, 0:128], a["norm1_g"].rearrange("l (c p) -> (l c) p", p=P), "rows")
            small(vrow[V_CW:V_CW + 16, 128:256], a["conv_w"].rearrange("l j (c p) -> (l j c) p", p=P), "rows")
            small(vrow[V_CB:V_CB + 4, 128:256], a["conv_b"].rearrange("l (c p) -> (l c) p", p=P), "rows")
            small(vrow[V_MG:V_MG + 4, 128:256], a["m_norm_g"].rearrange("l (c p) -> (l c) p", p=P), "rows")
            small(vrow[V_SK:V_SK + 4, 128:256], a["m_skip"].rearrange("l (c p) -> (l c) p", p=P), "rows")
            small(vrow[V_DA:V_DA + 1, 128:256], a["da_norm_g"], "rows")
            small(vrow[V_LB:V_LB + 8, 128:256], a["hgrn_lb_2"].rearrange("l (c p) -> (l c) p", p=P), "rows")
            small(vrow[V_HG:V_HG + 1, 128:256], a["hgrn_onorm_g_2"], "rows")
            small(vrow[V_RG:V_RG + 4, 128:256], a["ret_onorm_g_2"].rearrange("l (c p) -> (l c) p", p=P), "rows")
            small(mqk[:, 0:512].rearrange("p (h n) -> p h n", h=NH), a["w_mq"][0].rearrange("h p n -> p h n"), "mweights")
            small(mqk[:, 512:1024].rearrange("p (h n) -> p h n", h=NH), a["w_mk"][0].rearrange("h p n -> p h n"), "mweights")
            small(wg, a["w_mgate"][0].rearrange("(c p) g -> p c g", p=P), "mweights")
            small(gbias[0:NH, :], bass.AP(a["b_mgate"].tensor, 0, [[1, NH], [NH, 2]]), "mweights")
            small(lamq[0:64, :], bass.AP(a["lambda_qk"].tensor, 0, [[1, 64], [64, 4]]), "mweights")
            pool.memset(relb[32:33, :], NEG).then_inc(sig("relb_neg"), 1)
            small(relb[0:32, :], a["rel_bias"], "relb")
            w.more("bias_rows")
            pool.dma_start(scratch_dram, brow[0:NH, :].unsqueeze(1).broadcast_to([NH, P, 384])).then_inc(sig("bias_stored"), 16)
            pool.wait_ge(sig("bias_stored"), 16)
            small(btile, bass.AP(scratch_dram.tensor, P - 1, [[384 - 1, P], [P * 384, NH], [1, T]]), "btile")
            w.more("btile_used")
            gain(a["norm2_g"], 0)
            small(wr[:, :, 0:4], a["w_rg"][0].rearrange("(c p) g -> p c g", p=P), "router")
            small(wr[:, :, 4:36], a["w_re"][0].rearrange("(c p) g j -> p c (g j)", p=P), "router")
            small(br[:, 0:4], bass.AP(a["b_rg"].tensor, 0, [[0, P], [1, 4]]), "router")
            small(br[:, 4:36], bass.AP(a["b_re"].tensor, 0, [[0, P], [1, 32]]), "router")
            w.more("gain_free")
            gain(a["normf_g"], 0)

            def onehots(i, nxt):
                n = 0 if i is None else i * 3 + 1
                pool.tensor_copy(now[:, 0:2], pos_all[:, :, bass.ds(nxt, 1)]).then_inc(sig("now"), 1)
                if i is not None:
                    pool.tensor_copy(now[:, 2:4], pos_all[:, :, bass.ds(i, 1)]).then_inc(sig("now"), 1)
                    pool.tensor_copy(now[:, 4:6], gate_all[:, :, bass.ds(i, 1)]).then_inc(sig("now"), 1)
                    pool.wait_ge(sig("now"), n + 3)
                    pool.sem_inc(sig("now_seen"), 1)
                else:
                    pool.wait_ge(sig("now"), 1)
                for t in range(NT):
                    pool.tensor_scalar(sel[:, t, :], cst("slot")[:, 0:CAP], now[:, t:t + 1], 1.0,
                                       ALU.is_equal, ALU.mult).then_inc(sig("sel_ready"), 1)
                if i is None:
                    return
                for t in range(NT):
                    pool.tensor_scalar(selg[:, t, :], cst("slot"), now[:, 2 + t:3 + t], now[:, 4 + t:5 + t],
                                       ALU.is_equal, ALU.mult).then_inc(sig("selg_ready"), 1)

            w.more("positions_ready")
            onehots(None, 0)
            pool.wait_ge(sig("rounds_ready"), 1)
            nr = pool.value_load(nrounds_i[0:1, 0:1], min_val=0, max_val=ROUNDS - 1)
            with pool.Fori(0, nr * E + E) as i:
                pool.wait_ge(sig("gathered"), i + 1)
                pool.wait_ge(sig("selT_done"), i + 1)
                pool.sem_inc(sig("now_seen"), 1)
                onehots(i, i + 1)
            small(cB[:, :], a["consts_second"], "consts")
            for l in range(2):
                w.more("gain_free")
                gain(a["norm_g_2"], (l * 7 + 1) * D)
                if l == 0:
                    pos_dst = arena[:, 7168:7424].bitcast(I32)
                else:
                    pos_dst = scr[:, 512:768].bitcast(I32)
                w.more("pos_space")
                small(pos_dst, bass.AP(a["positions_2"].tensor, 0, [[0, P], [1, T]]), "pos")
                if l == 0:
                    small(sinks, bass.AP(a["attn_sinks_2"].tensor, 0, [[0, P], [1, 8]]), "pos")
                else:
                    small(cB[:, 0:DECAYS.shape[1]], a["decays"], "pos")
                w.more("gain_free")
                gain(a["norm_g_2"], (l * 7 + 3) * D)
                if l == 1:
                    for b in range(8):
                        w.more("out_high")
                        pool.tensor_tensor(al[:, 2 * b:2 * b + 2, :].rearrange("p c t -> p (c t)"), go[:, b * 512:(b + 1) * 512],
                                           rd[:, 2 * b:2 * b + 2, :].rearrange("p c t -> p (c t)"), ALU.subtract).then_inc(sig("act_ready"), 1)
                w.more("gain_free")
                gain(a["norm_g_2"], (l * 7 + 5) * D)
                small(arena[:, 2048:2560].rearrange("p (t n) -> p t n", t=NT),
                      a["p_2"][l].rearrange("b (t p) n -> p (b t) n", p=P), "p_loaded")
                w.more("gain_free")
                gain(a["norm_g_2"], (l * 7 + 6) * D)

        def diff_out(w, mm, pe, h):
            w.more("weights_ready")
            for t in range(3):
                last = pe.transpose(acc[:, 2, t * P:(t + 1) * P], dmix[:, t * P:(t + 1) * P], ident)
            last.then_inc(sig("weights_turned_psum"), 1)
            w.more("weights_turned")
            if h >= 2:
                w.more("heads_copied")
            b = acc[:, 3, (h % 2) * T:(h % 2 + 1) * T]
            v0, v1 = vd[:, 0, h * P:(h + 1) * P], vd[:, 1, h * P:(h + 1) * P]
            mm(b[:, 0:P], dmixT[:, 0:P], v0)
            mm(b[:, P:T], dmixT[:, P:2 * P], v0, True, False)
            mm(b[:, P:T], dmixT[:, 2 * P:3 * P], v1, False, True).then_inc(sig("heads_ready"), 1)

        @block.tensor
        def _(pe):
            w = Waits(pe)

            def mm(out, lhs, rhs, start=True, stop=True):
                return pe.matmul(out, lhs, rhs, start=start, stop=stop, skip_group_check=True)

            def mm3(out, lh, ll, rh, rl, start, stop):
                mm(out, lh, rh, start, False)
                mm(out, lh, rl, False, False)
                return mm(out, ll, rh, False, stop)

            def unit_ready(ep, u, it=0, per=0):
                pe.wait_ge(sig(f"{ep}_lo"), per * it + (u + 1))

            def features(ep, u, bank, lo=0, n=2, it=0, per=0):
                unit_ready(ep, u, it, per)
                s = u % RING
                for m in range(lo, lo + n):
                    for k in range(KC):
                        c = k * 256 + m * P
                        last = mm3(pw[:, bank, (m - lo) * T:(m - lo + 1) * T], wh[:, s, c:c + P], wl[:, s, c:c + P],
                                   ah[:, k, :], al[:, k, :], k == 0, k == KC - 1)
                return last

            def tokens(ep, u, bank, c0=0, n=256, at=0):
                unit_ready(ep, u)
                s = u % RING
                for t in range(NT):
                    for k in range(KC):
                        last = mm3(pw[:, bank, at + t * n:at + (t + 1) * n], ah[:, k, t * P:(t + 1) * P],
                                   al[:, k, t * P:(t + 1) * P], wh[:, s, k * 256 + c0:k * 256 + c0 + n],
                                   wl[:, s, k * 256 + c0:k * 256 + c0 + n], k == 0, k == KC - 1)
                return last

            def rows(ep, u, chunk, start, stop, it=0, per=0, final=False):
                unit_ready(ep, u, it, per)
                s = u % RING
                order = [(kk, t) for kk in range(2) for t in range(NT)]
                for kk, t in sorted(order, key=lambda a_: a_[1]) if final else order:
                    for half in range(2):
                        c = kk * D + half * 512
                        last = mm3(acc[:, 2 * t + half, :], ah[:, chunk + kk, t * P:(t + 1) * P],
                                   al[:, chunk + kk, t * P:(t + 1) * P], wh[:, s, c:c + 512], wl[:, s, c:c + 512],
                                   start and kk == 0, stop and kk == 1)
                    if final and (kk, t) == (1, 0):
                        last.then_inc(sig("first_tile"), 1)
                return last.then_inc(sig(f"{ep}_used"), 1)

            def turn_tokens(src, name, xn_signals):
                if xn_signals:
                    w.more(name, xn_signals)
                for c in range(KC):
                    for t in range(NT):
                        last = pe.transpose(pw[:, c // 2, (c % 2) * T + t * P:(c % 2) * T + (t + 1) * P],
                                            src[:, t, c * P:(c + 1) * P], ident)
                    if c % 2:
                        last.then_inc(sig("turned"), 1)

            xn = scr[:, :].rearrange("p (t d) -> p t d", t=NT)

            pe.sem_inc(sig("a_used"), RING)
            w.more("consts", 32)
            w.more("rows", 160)
            for k in range(2):
                last = pe.transpose(acc[:, 2, k * P:(k + 1) * P], vrow[:, k * P:(k + 1) * P], ident)
            last.then_inc(sig("psum_for_act"), 1)
            turn_tokens(xn, "xn_ready", 2)
            w.more("act_ready", 8)

            def project(u):
                if u >= 4:
                    w.more("proj_evac")
                last = features("a", u, u % 4) if u < 10 else tokens("a", u, u % 4)
                last.then_inc(sig("a_used"), 1)

            for u in range(4):
                project(u)
            w.more("relb", 16)
            w.more("relb_neg")
            mm(acc[0:NH, 3, 0:384], relb[0:33, :], cst("buckets")[0:33, :]).then_inc(sig("psum_for_dve"), 1)
            w.more("lam_prod")
            mm(acc[:, 1, 16:18], cst("mask3")[0:64, P:2 * P], sm[0:64, 88:90]).then_inc(sig("psum_for_act"), 1)
            for u in range(4, 7):
                project(u)
            w.more("mweights", 80)
            w.more("cact")
            for j in range(2):
                for h in range(NH):
                    last = mm(acc[:, 2 * j + h // 2, (h % 2) * T:(h % 2 + 1) * T], mqk[:, (j * NH + h) * P:(j * NH + h + 1) * P],
                              cact[:, h * T:(h + 1) * T])
            last.then_inc(sig("qk_psum"), 1)
            for u in range(7, 10):
                project(u)
            w.more("qm")
            w.more("km")
            for j in range(2):
                for c in range(12):
                    src = (qm, km, pF[:, F_V:F_V + 1024])[c // 4][:, (c % 4) * T:(c % 4 + 1) * T]
                    last = mm(acc[0:NH, 0, j * T:(j + 1) * T], wg[:, c, j * NH:(j + 1) * NH], src, c == 0, c == 11)
            last.then_inc(sig("psum_for_dve"), 1)
            for t in range(NT):
                for h in range(NH):
                    last = pe.transpose(acc[:, 2 + t, h * P:(h + 1) * P],
                                        pF[:, F_V + h * T + t * P:F_V + h * T + (t + 1) * P], ident)
            last.then_inc(sig("psum_for_act"), 1)
            project(10)
            project(11)
            w.more("proj_evac", 4)
            w.more("gate_rows")
            for t in range(NT):
                pe.transpose(acc[:, 1, t * 4:t * 4 + 4], a_row[:, t * P:(t + 1) * P], ident[0:NH, 0:NH])
                pe.transpose(acc[:, 1, 8 + t * 4:12 + t * 4], nm_row[:, t * P:(t + 1) * P], ident[0:NH, 0:NH])
            w.more("vt1", 2)
            for h in range(NH):
                last = mm(acc[:, 2 + h // 2, (h % 2) * T:(h % 2 + 1) * T], cst(f"sel{h}")[0:NH, :], mx_row)
            last.then_inc(sig("psum_for_dve"), 1)

            def scores(h):
                if h >= 2:
                    w.more("pairs_used")
                b = pw[:, h % 2, :]
                mm(b[:, 0:T], km[:, h * T:h * T + P], qm[:, h * T:(h + 1) * T])
                mm(b[:, T:T + P], km[:, h * T + P:(h + 1) * T], qm[:, h * T + P:(h + 1) * T]).then_inc(sig("pairs_ready"), 1)

            scores(0)
            scores(1)
            for h in range(NH):
                if h + 2 < NH:
                    scores(h + 2)
                w.more("weights_ready")
                if h >= 2:
                    w.more("heads_copied")
                b, wt = pw[:, 2 + h % 2, :], mw[h % 2]
                mm(b[:, 0:129], wt[:, 0:P], vt1[:, 0, h, :])
                mm(b[:, 129:258], wt[:, P:T], vt1[:, 0, h, :], True, False)
                mm(b[:, 129:258], wt[:, T:T + P], vt1[:, 1, h, :], False, True).then_inc(sig("heads_ready"), 1)
            w.passed("pairs_used", 2)
            w.more("heads_copied", 2)

            def turn_heads(src, dst):
                w.more("heads_normed")
                for h in range(NH):
                    for t in range(NT):
                        last = pe.transpose(dst[:, h // 2, (h % 2) * T + t * P:(h % 2) * T + (t + 1) * P],
                                            src[:, t, h, :], ident)
                last.then_inc(sig("heads_turned"), 1)

            def diff_logits(h):
                for c in range(2):
                    b = pw[:, 2 * (h % 2) + c, :]
                    if h >= 2 and c == 0:
                        w.more("pairs_used")
                    q = pF[64 * c:64 * c + 64, F_Q + h * T:F_Q + (h + 1) * T]
                    k = pF[64 * c:64 * c + 64, F_K + h * T:F_K + (h + 1) * T]
                    mm(b[:, 0:P], q[:, 0:P], k[:, 0:P])
                    last = mm(b[:, P:P + T], q[:, P:T], k)
                last.then_inc(sig("pairs_ready"), 1)

            diff_logits(0)
            diff_logits(1)
            turn_heads(ob, acc[:, 0:2, :])
            for h in range(2, NH):
                diff_logits(h)
                diff_out(w, mm, pe, h - 2)
            diff_out(w, mm, pe, NH - 2)
            diff_out(w, mm, pe, NH - 1)
            w.passed("pairs_used", 2)
            w.more("heads_copied", 2)
            w.more("act_ready", 4)
            rows("a", 12, 0, True, False)
            rows("a", 13, 2, False, False)
            turn_heads(ob2, pw[:, 0:2, :])
            w.more("act_ready", 4)
            rows("a", 14, 4, False, False)
            rows("a", 15, 6, False, True)
            pe.wait_ge(sig("a_used"), NA + RING)
            pe.sem_inc(sig("m_used"), RING)
            turn_tokens(h2, "h2_ready", 2)
            w.more("h2T", 4)
            w.more("router", 64)
            for t in range(NT):
                for c in range(KC):
                    last = mm(acc[:, 0, t * 36:(t + 1) * 36], h2T[:, c, t * P:(t + 1) * P], wr[:, c, :], c == 0, c == KC - 1)
            last.then_inc(sig("psum_for_dve"), 1)
            w.more("masks")
            ones = cst("mask3")[:, P:2 * P]
            mm(acc[:, 1, 0:32], cst("before"), masks[:, 0, :])
            mm(acc[:, 1, 32:64], cst("before"), masks[:, 1, :], True, False)
            mm(acc[:, 1, 32:64], ones, masks[:, 0, :], False, True)
            mm(acc[:, 1, 64:96], ones, masks[:, 0, :], True, False)
            mm(acc[:, 1, 64:96], ones, masks[:, 1, :], False, True).then_inc(sig("psum_for_dve"), 1)

            def zero(bank):
                return mm(bank.rearrange("p (a n) -> p a n", a=4), zr[:, :], zr[:, :].unsqueeze(1).broadcast_to([P, 4, P]), True, False)

            def gather(bank):
                for k in range(4 * bank, 4 * bank + 4):
                    for part, src in enumerate((h2h, h2l)):
                        c = (k % 4) * P + part * CAP
                        for t in range(NT):
                            last = mm(pw[:, bank, c:c + CAP], src[:, t, k, :], sel[:, t, :], t == 0, t == 1)
                last.then_inc(sig("gathered_low" if bank == 0 else "gathered"), 1)

            def scatter(t, half):
                for part in (ydh, ydl):
                    last = mm(acc[:, 2 * t + half, :], selT[:, t * P:(t + 1) * P], part[:, half * 512:(half + 1) * 512], False, False)
                return last

            w.more("zr")
            zero(acc[:, 2, :])
            zero(acc[:, 3, :])
            w.more("positions_read")
            zero(acc[:, 0, :])
            zero(acc[:, 1, :])
            w.more("h2_split", 2)
            w.more("sel_ready", 2)
            gather(0)
            gather(1)
            pe.wait_ge(sig("xg_ready"), 2)
            pe.sem_inc(sig("selT_done"), 1)
            pe.wait_ge(sig("rounds_ready"), 1)
            nr = pe.value_load(nrounds_i[0:1, 0:1], min_val=0, max_val=ROUNDS - 1)
            with pe.Fori(0, nr * E + E) as i:
                pe.wait_ge(sig("xg_ready"), i * 2 + 2)
                for j in range(4):
                    if j == 2:
                        pe.wait_ge(sig("selT_ready"), i * 2 + 2)
                    unit_ready("m", j, i, 6)
                    for kk in range(4):
                        k = 4 * (j % 2) + kk
                        for part in (wh, wl):
                            last = mm(pw[:, 2 + j // 2, :], xg[:, k, :], part[:, j % RING, kk * 512:(kk + 1) * 512],
                                      k == 0 and part is wh, k == KC - 1 and part is wl)
                    last.then_inc(sig("m_used"), 1)
                pe.wait_ge(sig("sel_ready"), i * 2 + 4)
                pe.wait_ge(sig("yd_ready"), i + 1)
                gather(0)
                scatter(0, 0)
                scatter(0, 1)
                pe.wait_ge(sig("gus_ready"), i * 2 + 2)
                for gu in range(2):
                    for c in range(4):
                        last = mm(pw[:, 2, (gu * 4 + c) * CAP:(gu * 4 + c + 1) * CAP],
                                  gus[:, gu * 512 + c * P:gu * 512 + (c + 1) * P], cst("fold"))
                last.then_inc(sig("folded"), 1)
                scatter(1, 0)
                gather(1)
                pe.wait_ge(sig("selg_ready"), i * 2 + 2)
                for t in range(NT):
                    last = pe.transpose(pw[:, 3, t * P:(t + 1) * P], selg[:, t, :], ident)
                last.then_inc(sig("selT_done"), 1)
                scatter(1, 1).then_inc(sig("scattered"), 1)
                pe.wait_ge(sig("xg_ready"), i * 2 + 4)
                pe.wait_ge(sig("hid_ready"), i + 1)
                for j in range(4, 6):
                    unit_ready("m", j, i, 6)
                    for cc in range(2):
                        c = 2 * (j - 4) + cc
                        for half in range(2):
                            for part in (wh, wl):
                                last = mm(pw[:, half, :], hid[:, c, :],
                                          part[:, j % RING, cc * D + half * 512:cc * D + (half + 1) * 512],
                                          c == 0 and part is wh, c == 3 and part is wl)
                    last.then_inc(sig("m_used"), 1)
            total = nr * E + E
            pe.wait_ge(sig("selT_ready"), total * 2 + 2)
            pe.wait_ge(sig("yd_ready"), total + 1)
            scatter(0, 0)
            scatter(0, 1)
            scatter(1, 0)
            scatter(1, 1).then_inc(sig("scattered"), 1)
            pe.wait_ge(sig("m_used"), total * 6 + RING)
            pe.sem_inc(sig("b_used"), RING)
            def keep_clock(n):
                for _ in range(n):
                    zero(pw[:, 3, :])

            def turn_normed(idle=19):
                keep_clock(idle)
                for t in range(NT):
                    w.more("diag_ready")
                    for c in range(KC):
                        last = mm(pw[:, c // 2, (c % 2) * T + t * P:(c % 2) * T + (t + 1) * P],
                                  x[:, t, c * P:(c + 1) * P], diag[:, t, :])
                        if t == NT - 1 and c % 2:
                            last.then_inc(sig("turned"), 1)

            def ffn(l, n, idx):
                u0, done = UB[(l, f"ffn{n}")], idx * FB
                turn_normed()
                for b in range(4):
                    zero(acc[:, b, :])
                w.more("act_ready", 8)
                features("b", u0, 0).then_inc(sig("b_used"), 1)
                features("b", u0 + 1, 1).then_inc(sig("b_used"), 1)
                with pe.Fori(0, 5) as it:
                    for par in range(2):
                        u = u0 + 2 + 3 * par
                        features("b", u, 2 * (1 - par), it=it, per=6).then_inc(sig("b_used"), 1)
                        features("b", u + 1, 2 * (1 - par) + 1, it=it, per=6).then_inc(sig("b_used"), 1)
                        pe.wait_ge(sig("ff_ready"), it * 2 + (done + par + 1))
                        rows("b", u + 2, 8 + 2 * par, False, False, it=it, per=6)
                pe.wait_ge(sig("ff_ready"), done + FB)
                rows("b", u0 + 32, 8, False, True, final=True)

            def ple(l):
                turn_tokens(x, "x_ready", 1)
                w.more("p_loaded", 16)
                for c in range(2):
                    for t in range(NT):
                        last = pe.transpose(acc[:, 0, c * T + t * P:c * T + (t + 1) * P], pt[:, t, c * P:(c + 1) * P], ident)
                last.then_inc(sig("psum_for_act"), 1)
                w.more("act_ready", 9)
                for j in range(4):
                    rows("b", UB[(l, "ple_gate")] + j, 2 * j, j == 0, j == 3)
                w.more("ple_gate", 2)
                rows("b", UB[(l, "ple_proj")], 8, True, True, final=True)

            def even():
                u0 = UB[(0, "mix_in")]
                turn_normed()
                w.more("act_ready", 8)
                for j in range(11):
                    if j >= 4:
                        w.more("proj_evac")
                    if j in (4, 5):
                        last = tokens("b", u0 + j, j % 4)
                    elif j < 10:
                        last = features("b", u0 + j, j % 4)
                    else:
                        features("b", u0 + j, j % 4, 0, 1)
                        last = tokens("b", u0 + j, j % 4, P, P, T)
                    last.then_inc(sig("b_used"), 1)
                w.more("proj_evac", 4)
                for c in range(4):
                    mm(acc[:, c // 2, (c % 2) * T:(c % 2 + 1) * T], cst("rot"), qb[:, c * T:(c + 1) * T])
                for g in range(2):
                    mm(acc[:, 2, g * T:(g + 1) * T], cst(f"dup{g}"), kb)
                    last = mm(acc[:, 3, g * T:(g + 1) * T], cst(f"duprot{g}"), kb)
                last.then_inc(sig("psum_for_dve"), 1)
                w.more("roped")

                def logits(h):
                    if h >= 2:
                        w.more("pairs_used")
                    rows_ = slice(64 * (h % 2), 64 * (h % 2) + 64)
                    q, k, g = qr[rows_, (h // 2) * T:(h // 2 + 1) * T], kr[rows_, :], h // 4
                    b = pw[:, h % 2, :]
                    mm(b[:, 0:P], q[:, 0:P], k[:, g * T:g * T + P])
                    mm(b[:, P:P + T], q[:, P:T], k[:, g * T:(g + 1) * T]).then_inc(sig("pairs_ready"), 1)

                logits(0)
                logits(1)
                for h in range(8):
                    if h + 2 < 8:
                        logits(h + 2)
                    w.more("weights_ready")
                    b = acc[:, h % 2, :]
                    for j in range(3):
                        last = pe.transpose(b[:, j * P:(j + 1) * P], swl[h % 2][:, j * P:(j + 1) * P], ident)
                    last.then_inc(sig("weights_turned_psum"), 1)
                    w.more("weights_turned")
                    c, g, pT = h // 2, h // 4, swt[h % 2]
                    out = pw[64 * (h % 2):64 * (h % 2) + 64, 2 + c // 2, (c % 2) * T:(c % 2 + 1) * T]
                    mm(out[:, 0:P], vb[:, 0, g * 64:g * 64 + 64], pT[:, 0:P])
                    mm(out[:, P:T], vb[:, 0, g * 64:g * 64 + 64], pT[:, P:T], True, False)
                    last = mm(out[:, P:T], vb[:, 1, g * 64:g * 64 + 64], pT[:, T:T + P], False, True)
                    if h % 4 == 3:
                        last.then_inc(sig("sw_out"), 1)
                w.passed("pairs_used", 2)
                w.more("hgrn_ready")

                def pairs(h):
                    if h >= 2:
                        w.more("pairs_used")
                    b = pw[:, h % 2, :]
                    q = qs[:, h * T:(h + 1) * T]
                    for m in range(4):
                        for n in range(2 * (m // 2), 4):
                            if n <= m:
                                lhs = ks[:, h * T + m * 64:h * T + m * 64 + 64]
                            elif n == m + 1:
                                lhs = kd[:, h * T + m * 64:h * T + m * 64 + 64]
                            else:
                                v = {(0, 2): 0, (0, 3): 1, (1, 3): 2}[(m, n)]
                                lhs = eb[:, v * T + h * 64:v * T + h * 64 + 64]
                            c = n * 64 + (P if m >= 2 else 0)
                            last = mm(b[64 * (m % 2):64 * (m % 2) + 64, c:c + 64], lhs, q[:, n * 64:n * 64 + 64])
                    last.then_inc(sig("pairs_ready"), 1)

                pairs(0)
                pairs(1)
                w.more("act_ready", 2)
                for h in range(NH):
                    if h + 2 < NH:
                        pairs(h + 2)
                    w.more("weights_ready")
                    if h >= 2:
                        w.more("heads_copied")
                    b, wt = pw[:, 2 + h % 2, :], swl[h % 2]
                    v0, v1 = ia[:, 0, h * P:(h + 1) * P], ia[:, 1, h * P:(h + 1) * P]
                    mm(b[:, 0:P], wt[:, 0:P], v0)
                    mm(b[:, P:T], wt[:, P:T], v0, True, False)
                    mm(b[:, P:T], wt[:, T:T + P], v1, False, True).then_inc(sig("heads_ready"), 1)
                w.passed("pairs_used", 2)
                w.more("heads_copied", 2)
                o0 = UB[(0, "mix_out")]
                rows("b", o0, 4, True, False)
                rows("b", o0 + 1, 6, False, False)
                turn_heads(oh, pw[:, 0:2, :])
                w.more("act_ready", 4)
                rows("b", o0 + 2, 0, False, False)
                rows("b", o0 + 3, 2, False, True, final=True)

            def odd():
                u0 = UB[(1, "mix_in")]
                turn_normed()
                w.more("act_ready", 8)
                for j in range(24):
                    if j >= 4:
                        w.more("proj_evac")
                    last = tokens("b", u0 + j, j % 4) if 8 <= j < 16 else features("b", u0 + j, j % 4)
                    last.then_inc(sig("b_used"), 1)
                w.more("proj_evac", 4)
                w.more("roped")

                def pairs(h):
                    if h >= 2:
                        w.more("pairs_used")
                    b = pw[:, h % 2, :]
                    for part, (s0, c0, n) in enumerate(((0, 0, T), (P, T, P))):
                        for cc in range(2):
                            k = arena[:, 2048 + (2 * h + cc) * T + s0:2048 + (2 * h + cc) * T + s0 + P]
                            q = arena[:, (2 * h + cc) * T + T - n:(2 * h + cc + 1) * T]
                            last = mm(b[:, c0:c0 + n], k, q, cc == 0, cc == 1)
                    last.then_inc(sig("pairs_ready"), 1)

                pairs(0)
                pairs(1)
                for h in range(NH):
                    if h + 2 < NH:
                        pairs(h + 2)
                    w.more("weights_ready")
                    if h >= 1:
                        w.more("ro_copied", 2)
                    wt = ratt[h % 2]
                    v0, v1 = vo[:, 0, h * 512:(h + 1) * 512], vo[:, 1, h * 512:(h + 1) * 512]
                    mm(pw[:, 2, :], wt[:, 0:P], v0)
                    mm(pw[:, 3, :], wt[:, P:T], v0, True, False)
                    mm(pw[:, 3, :], wt[:, T:T + P], v1, False, True).then_inc(sig("heads_ready"), 1)
                w.passed("pairs_used", 2)
                w.more("ro_copied", 2)
                for c in range(16):
                    if c % 4 == 0:
                        w.more("heads_normed")
                    for t in range(NT):
                        src = oo[:, t * 4 + c // 4, (c % 4) * P:(c % 4 + 1) * P]
                        if c >= 8 and c % 2 == 0 and t == 0:
                            w.more("ry", 2)
                        last = pe.transpose(pw[:, (c // 2) % 4, (c % 2) * T + t * P:(c % 2) * T + (t + 1) * P], src, ident)
                    if c % 2:
                        last.then_inc(sig("ro_turned"), 1)
                w.passed("ry", 8)
                for j in range(8):
                    w.more("act_ready")
                    rows("b", UB[(1, "mix_out")] + j, 2 * j, j == 0, j == 7, final=j == 7)

            for l in range(2):
                ffn(l, 1, 2 * l)
                if l == 0:
                    w.more("consts", 16)
                    even()
                else:
                    odd()
                ffn(l, 2, 2 * l + 1)
                ple(l)

        def num_copy(w, act, h):
            w.more("heads_ready")
            src = pw[:, 2 + h % 2, 0:258].rearrange("p (t d) -> p t d", t=NT)
            act.activation(sm[:, 32:40].rearrange("p (t h) -> p t h", t=NT)[:, :, h:h + 1], src[:, :, P:P + 1],
                           ACT.Copy).then_inc(sig("den_copied"), 1)
            act.wait_ge(sig("den_copied"), h + 1)
            act.activation(ob[:, :, h, :], src[:, :, 0:P], ACT.Copy).then_inc(sig("heads_copied"), 1)

        @block.scalar
        def _(act):
            w = Waits(act)

            def split(ep, u, it=0, per=0):
                act.wait_ge(sig(f"{ep}_landed{u % RING}"), 16 * ((per // RING) * it + (u // RING + 1)))
                act.activation(wh[:, u % RING, :], raw[:, u % RING, :], ACT.Copy).then_inc(sig(f"{ep}_hi"), 1)

            def used(ep, u, it=0, per=0):
                act.wait_ge(sig(f"{ep}_used"), per * it + (u + 1 + RING))

            def rms(scale=1.0, bias=0.0, src=None, n=2):
                w.more("meansq_ready")
                act.activation(sm[:, 12:12 + n], sm[:, 10:10 + n] if src is None else src, ACT.Sqrt,
                               scale=scale, bias=bias).then_inc(sig("rms_ready"), 1)

            def norm_in(col):
                rms()
                w.more("rstd_ready")
                act.activation(scr[:, D:2 * D], x[:, 1, :], ACT.Copy, scale=sm[:, 15:16]).then_inc(sig("xn_ready"), 1)
                highs(col, KC)

            def highs(col, n, chunk=0):
                for c in range(n):
                    if c % 2 == 0:
                        w.more("turned")
                    src = pw[:, c // 2, (c % 2) * T:(c % 2 + 1) * T]
                    act.activation(ah[:, chunk + c, :], src, ACT.Copy, scale=1.0 if col is None else col(c)).then_inc(sig("high"), 1)

            def silu_table():
                act.activation(sm[:, 170:171], cst("tie")[:, 0:1], ACT.Silu)

            def sqrt_table():
                act.activation(sm[:, 171:172], cst("tie")[:, 0:1], ACT.Sqrt)

            rms()
            w.more("rstd_ready")
            act.activation(scr[:, D:2 * D], x[:, 1, :], ACT.Copy, scale=sm[:, 15:16]).then_inc(sig("xn_ready"), 1)
            w.more("psum_for_act")
            act.activation(vcol[:, :], acc[:, 2, 0:T], ACT.Copy).then_inc(sig("vcol"), 1)
            w.more("vcol")
            highs(lambda c: vcol[:, 112 + c:113 + c], KC)

            def evac_in(u):
                used("a", u)
                src = pw[:, u % 4, :]
                if u in (4, 5):
                    act.activation(pF[:, u * 512:(u + 1) * 512], src, ACT.Sigmoid).then_inc(sig("proj_evac"), 1)
                elif u < 10:
                    act.activation(pF[:, u * 512:(u + 1) * 512], src, ACT.Copy).then_inc(sig("proj_evac"), 1)
                else:
                    act.activation(vd[:, :, (u - 10) * 256:(u - 9) * 256], src.rearrange("p (t n) -> p t n", t=NT),
                                   ACT.Copy).then_inc(sig("proj_evac"), 1)

            for u in range(12):
                split("a", u)
                if u >= 2:
                    evac_in(u - 2)
                if u == 6:
                    w.more("psum_for_act")
                    act.activation(sm[:, 90:92], acc[:, 1, 16:18], ACT.Exp).then_inc(sig("act_result"), 1)
                    w.more("dve_result")
                    act.activation(cact, cact, ACT.Silu).then_inc(sig("cact"), 1)
                if u == 9:
                    w.more("qk_psum")
                    act.activation(qm.rearrange("p (b n) -> p b n", b=2), acc[:, 0:2, :], ACT.Copy).then_inc(sig("qm"), 1)
            w.more("dve_result")
            act.activation(scr[0:NH, 1024:1280], scr[0:NH, 1280:1536], ACT.Exp, scale=-1.0).then_inc(sig("gate_exp"), 1)
            w.more("gate_exp")
            act.activation(scr[0:NH, 1280:1536], scr[0:NH, 1024:1280], ACT.Ln, bias=1.0).then_inc(sig("act_result"), 1)
            w.more("psum_for_act")
            act.activation(vt1[:, :, :, 0:P], acc[:, 2:4, :].rearrange("p t (h d) -> p t h d", h=NH), ACT.Copy).then_inc(sig("vt1"), 1)
            split("a", 12)
            evac_in(10)
            split("a", 13)
            evac_in(11)
            split("a", 14)
            w.more("gate_cols")
            act.activation(sm[:, 24:32], sm[:, 24:32], ACT.Exp).then_inc(sig("floor"), 1)
            for h in range(NH):
                w.more("exponents_ready")
                e = scr[:, 768 + 384 * (h % 2):768 + 384 * (h % 2 + 1)]
                act.activation(e, e, ACT.Exp, scale=-1.0).then_inc(sig("exponentials"), 1)
                if h >= 1:
                    num_copy(w, act, h - 1)
            num_copy(w, act, NH - 1)
            w.more("dve_result")
            act.activation(sm[:, 72:80], sm[:, 64:72], ACT.Sqrt).then_inc(sig("act_result"), 1)
            for h in range(NH):
                w.more("head_gated")
                act.activation(ah[:, h, :], arena[:, F_C + h * T:F_C + (h + 1) * T], ACT.Copy).then_inc(sig("high"), 1)
            def diff_copies(h):
                w.more("weights_turned_psum")
                act.activation(dmixT, acc[:, 2, 0:384], ACT.Copy).then_inc(sig("weights_turned"), 1)
                w.more("heads_ready")
                act.activation(ob2[:, :, h, :], acc[:, 3, (h % 2) * T:(h % 2 + 1) * T].rearrange("p (t d) -> p t d", t=NT),
                               ACT.Copy).then_inc(sig("heads_copied"), 1)

            for h in range(NH):
                w.more("exponents_ready", 2)
                for c in range(2):
                    k = 96 + 4 * (h % 2) + c
                    lo = dlog[h % 2]
                    act.activation(lo[:, c, 0:P], lo[:, c, 0:P], ACT.Exp, bias=sm[:, k:k + 1],
                                   accum_out=sm[:, k + 8:k + 9]).then_inc(sig("exponentials"), 1)
                    act.activation(lo[:, c, P:P + T], lo[:, c, P:P + T], ACT.Exp, bias=sm[:, k + 2:k + 3],
                                   accum_out=sm[:, k + 10:k + 11]).then_inc(sig("exponentials"), 1)
                if h >= 1:
                    diff_copies(h - 1)
            diff_copies(NH - 1)
            w.more("dve_result")
            act.activation(sm[:, 72:80], sm[:, 64:72], ACT.Sqrt).then_inc(sig("act_result"), 1)
            w.more("heads_turned", 2)
            w.more("lam")
            for h in range(NH):
                act.activation(ah[:, 4 + h, :], pw[:, h // 2, (h % 2) * T:(h % 2 + 1) * T], ACT.Copy,
                               scale=sm[:, 93:94]).then_inc(sig("high"), 1)
            split("a", 15)
            sqrt_table()
            for t in range(NT):
                w.more("x_new")
                act.activation(junk1[:, t, :], x[:, t, :], ACT.Square, accum_out=sm[:, 10 + t:11 + t]).then_inc(sig("act_step"), 1)
            w.more("act_step", 2)
            act.activation(sm[:, 12:14], sm[:, 10:12], ACT.Sqrt, scale=1.0 / D, bias=sm[:, 168:169]).then_inc(sig("rms_ready"), 1)
            for b in range(4):
                w.more("turned")
                act.activation(h2T[:, 2 * b:2 * b + 2, :], pw[:, b, :].rearrange("p (c t) -> p c t", c=2), ACT.Copy).then_inc(sig("h2T"), 1)
            for t in range(NT):
                src = h2[:, t, :].rearrange("p (f k) -> p k f", k=KC)
                act.activation(h2h[:, t, :, :], src, ACT.Copy).then_inc(sig("h2_high"), 1)
            split("m", 0)
            split("m", 1)
            w.more("dve_result")
            act.activation(rt[:, 72:82], rt[:, 72:82], ACT.Exp).then_inc(sig("act_result"), 1)
            w.more("dve_result")
            act.activation(rt[:, 82:84], rt[:, 82:84], ACT.Exp).then_inc(sig("act_result"), 1)
            act.wait_ge(sig("gathered_low"), 1)
            act.activation(xg[:, 0:4, :], pw[:, 0, :].rearrange("p (k s) -> p k s", k=4), ACT.Copy).then_inc(sig("xg_ready"), 1)
            act.wait_ge(sig("rounds_ready"), 1)
            nr = act.value_load(nrounds_i[0:1, 0:1], min_val=0, max_val=ROUNDS - 1)
            silu_table()
            act.wait_ge(sig("xg_ready"), 2)
            act.wait_ge(sig("gathered"), 1)
            with act.Fori(0, nr * E + E) as i:
                split("m", 2, i, 6)
                split("m", 3, i, 6)
                act.wait_ge(sig("m_used"), i * 6 + RING)
                act.wait_ge(sig("selT_ready"), i * 2 + 2)
                act.activation(ydh.rearrange("p (b n) -> p b n", b=2), pw[:, 0:2, :], ACT.Copy, scale=slot_gate).then_inc(sig("yd_high"), 1)
                split("m", 4, i, 6)
                act.wait_ge(sig("m_used"), i * 6 + (2 + RING))
                act.activation(gus[:, 0:512], pw[:, 2, :], ACT.Copy).then_inc(sig("gus_ready"), 1)
                split("m", 5, i, 6)
                act.wait_ge(sig("m_used"), i * 6 + (4 + RING))
                act.activation(gus[:, 512:1024], pw[:, 3, :], ACT.Copy).then_inc(sig("gus_ready"), 1)
                split("m", 6, i, 6)
                act.wait_ge(sig("gathered_low"), i + 2)
                act.activation(xg[:, 0:4, :], pw[:, 0, :].rearrange("p (k s) -> p k s", k=4), ACT.Copy).then_inc(sig("xg_ready"), 1)
                act.wait_ge(sig("folded"), i + 1)
                act.activation(silu_s, pw[:, 2, 0:256], ACT.Silu).then_inc(sig("silu"), 1)
                act.wait_ge(sig("hid_s"), i + 1)
                act.activation(hid[:, :, 0:CAP], hid_s.rearrange("p (c s) -> p c s", c=4), ACT.Copy).then_inc(sig("hid_high"), 1)
                split("m", 7, i, 6)
            total = nr * E + E
            act.wait_ge(sig("m_used"), total * 6 + RING)
            act.wait_ge(sig("selT_ready"), total * 2 + 2)
            act.activation(ydh.rearrange("p (b n) -> p b n", b=2), pw[:, 0:2, :], ACT.Copy, scale=slot_gate).then_inc(sig("yd_high"), 1)
            act.wait_ge(sig("m_hi"), total * 6 + 2)
            act.sem_inc(sig("b_hi"), 2)
            act.sem_inc(sig("b_landed0"), 16)
            act.sem_inc(sig("b_landed1"), 16)
            rms()
            def ahead(u, n):
                for j in range(n):
                    split("b", u + j)

            def norm_in(col):
                sqrt_table()
                for t in range(NT):
                    w.more("x_new")
                    act.activation(junk[:, t, :], x[:, t, :], ACT.Square, accum_out=sm[:, 10 + t:11 + t]).then_inc(sig("act_step"), 1)
                    w.more("act_step")
                    act.activation(sm[:, 12 + t:13 + t], sm[:, 10 + t:11 + t], ACT.Sqrt, scale=1.0 / D,
                                   bias=eps_col(1.0)).then_inc(sig("rms_ready"), 1)
                highs(col, KC)

            def ffn(l, n, idx):
                u0, done = UB[(l, f"ffn{n}")], idx * FB
                norm_in(lambda c: norm_col(l, 4 * (n - 1), c))

                def activate(par, it, b):
                    act.wait_ge(sig("b_used"), it * 6 + (u0 + (3 * b + 1 if b else 2) + RING))
                    act.activation(scr[:, par * 512:(par + 1) * 512], pw[:, 2 * par, :], ACT.Silu).then_inc(sig("ff_silu"), 1)
                    act.wait_ge(sig("ff_hid"), it * 2 + (done + b + 1))
                    act.activation(ah[:, 8 + 2 * par:10 + 2 * par, :].rearrange("p c t -> p (c t)"),
                                   scr[:, 1024 + par * 512:1536 + par * 512], ACT.Copy).then_inc(sig("ff_high"), 1)

                silu_table()
                with act.Fori(0, 5) as it:
                    for par in range(2):
                        u = u0 + 2 + 3 * par
                        split("b", u, it, 6)
                        split("b", u + 1, it, 6)
                        activate(par, it, par)
                        split("b", u + 2, it, 6)
                split("b", u0 + 32)
                activate(0, 0, FB - 1)
                ahead(u0 + 33, 3)
                residual_rms(u0 + 32, 4.0)

            def residual_rms(u, factor):
                sqrt_table()
                for t in range(NT):
                    if u is None:
                        w.more("ple_y")
                        src = sg[:, t, :].rearrange("p (b n) -> p b n", b=2)
                    else:
                        src = acc[:, 2 * t:2 * t + 2, :]
                        if t == 0:
                            w.more("first_tile")
                        else:
                            used("b", u)
                    act.activation(junk[:, t, :].rearrange("p (b n) -> p b n", b=2), src,
                                   ACT.Square, accum_out=sm[:, 10 + t:11 + t]).then_inc(sig("squares"), 1)
                    w.more("squares")
                    act.activation(sm[:, 12 + t:13 + t], sm[:, 10 + t:11 + t], ACT.Sqrt, scale=factor / D,
                                   bias=eps_col(factor)).then_inc(sig("rms_ready"), 1)
                if u is None:
                    w.passed("first_tile")

            def eps_col(factor):
                return sm[:, 169:170] if factor == 4.0 else sm[:, 168:169]

            def trig(l):
                w.more("dve_result")
                _, _, cos, sin = rope[l]
                act.activation(sin, trig_in[l], ACT.Sin).then_inc(sig("act_result"), 1)
                act.activation(cos, trig_in[l], ACT.Sin, scale=0.5).then_inc(sig("act_result"), 1)

            def ple(l):
                w.passed("x_new", 2)
                highs(None, KC)
                w.more("psum_for_act")
                act.activation(ah[:, 8:10, :].rearrange("p c t -> p (c t)"), acc[:, 0, :], ACT.Copy).then_inc(sig("high"), 1)
                u0 = UB[(l, "ple_gate")]
                split("b", u0 + 3)
                split("b", u0 + 4)
                used("b", u0 + 3)
                for t in range(NT):
                    act.activation(sg[:, t, :].rearrange("p (b n) -> p b n", b=2), acc[:, 2 * t:2 * t + 2, :], ACT.Sigmoid).then_inc(sig("ple_gate"), 1)
                if l == 0:
                    ahead(u0 + 5, 2)
                residual_rms(None, 1.0)

            def even():
                u0 = UB[(0, "mix_in")]
                norm_in(lambda c: norm_col(0, 2, c))
                trig(0)
                w.more("dve_result")
                act.activation(sm[:, 124:128], sm[:, 120:124], ACT.Sigmoid).then_inc(sig("act_result"), 1)

                def evac(j):
                    used("b", u0 + j)
                    src = pw[:, j % 4, :]
                    tt = src.rearrange("p (t n) -> p t n", t=NT)
                    if j in (4, 5):
                        ins = act.activation(ia[:, :, (j - 4) * 256:(j - 3) * 256], tt, ACT.Copy)
                    elif j == 10:
                        act.activation(kb, src[:, 0:T], ACT.Copy).then_inc(sig("kb"), 1)
                        w.more("kb")
                        ins = act.activation(vb, src[:, T:2 * T].rearrange("p (t n) -> p t n", t=NT), ACT.Copy)
                    else:
                        c0 = j * 512 if j < 4 else (j - 2) * 512
                        func = {0: ACT.Silu, 1: ACT.Sigmoid, 3: ACT.Silu, 4: ACT.Copy}[j // 2]
                        ins = act.activation(arena[:, c0:c0 + 512], src, func)
                    ins.then_inc(sig("proj_evac"), 1)

                for j in range(3, 11):
                    split("b", u0 + j)
                    evac(j - 3)
                    if j == 7:
                        w.more("dve_result")
                        act.activation(kd, fk, ACT.Ln).then_inc(sig("act_result"), 1)
                    if j == 8:
                        w.more("dve_result")
                        b16 = bsum.rearrange("p (g c) -> p g c", c=64)
                        act.activation(eb, bsum, ACT.Exp).then_inc(sig("act_result"), 1)
                        act.activation(ks, bsum, ACT.Exp, scale=-1.0).then_inc(sig("act_result"), 1)
                        act.activation(sm[:, 136:152].unsqueeze(2), b16[:, :, 63:64], ACT.Exp).then_inc(sig("act_result"), 1)
                        w.more("dve_result")
                        act.activation(kd, kd, ACT.Exp).then_inc(sig("act_result"), 1)
                for j in range(8, 11):
                    evac(j)
                for j in range(4):
                    split("b", UB[(0, "mix_out")] + j)
                for h in range(8):
                    k = 96 + 8 * (h % 2)
                    w.more("exponents_ready")
                    for t, (c0, n) in enumerate(((0, P), (P, T))):
                        e = swl[h % 2][:, c0:c0 + n]
                        act.activation(e, e, ACT.Exp, bias=sm[:, k + t:k + t + 1], accum_out=sm[:, k + 2 + t:k + 3 + t]).then_inc(sig("exponentials"), 1)
                    act.activation(sm[:, k + 4:k + 6], sm[:, k:k + 2], ACT.Exp, bias=sinks[:, h:h + 1]).then_inc(sig("exponentials"), 1)
                    if h >= 1:
                        w.more("weights_turned_psum")
                        act.activation(swt[(h - 1) % 2], acc[:, (h - 1) % 2, 0:384], ACT.Copy).then_inc(sig("weights_turned"), 1)
                w.more("weights_turned_psum")
                act.activation(swt[1], acc[:, 1, 0:384], ACT.Copy).then_inc(sig("weights_turned"), 1)
                w.more("sw_out", 2)
                for b in range(2):
                    act.activation(ah[:, 4 + 2 * b:6 + 2 * b, :].rearrange("p c t -> p (c t)"), pw[:, 2 + b, :], ACT.Copy).then_inc(sig("high"), 1)
                for h in range(NH):
                    w.more("heads_ready")
                    act.activation(oh[:, :, h, :], pw[:, 2 + h % 2, 0:T].rearrange("p (t d) -> p t d", t=NT), ACT.Copy).then_inc(sig("heads_copied"), 1)
                w.more("dve_result")
                act.activation(sm[:, 72:80], sm[:, 64:72], ACT.Sqrt).then_inc(sig("act_result"), 1)
                for h in range(NH):
                    w.more("head_gated")
                    act.activation(ah[:, h, :], ga[:, h * T:(h + 1) * T], ACT.Copy).then_inc(sig("high"), 1)
                ahead(UB[(0, "ffn2")], 2)
                residual_rms(UB[(0, "mix_out")] + 3, 1.0)

            def odd():
                u0 = UB[(1, "mix_in")]
                norm_in(lambda c: norm_col(1, 2, c))
                trig(1)

                def evac(j):
                    used("b", u0 + j)
                    src = pw[:, j % 4, :]
                    if 8 <= j < 16:
                        ins = act.activation(vo[:, :, (j - 8) * 256:(j - 7) * 256], src.rearrange("p (t n) -> p t n", t=NT), ACT.Copy)
                    else:
                        c0 = j * 512 if j < 8 else 8192 + (j - 16) * 512
                        ins = act.activation(arena[:, c0:c0 + 512], src, ACT.Copy if j < 8 else ACT.Silu)
                    ins.then_inc(sig("proj_evac"), 1)

                for j in range(3, 24):
                    split("b", u0 + j)
                    evac(j - 3)
                for j in range(21, 24):
                    evac(j)
                o0 = UB[(1, "mix_out")]
                for j in range(4):
                    split("b", o0 + j)
                for h in range(NH):
                    w.more("heads_ready")
                    for t in range(NT):
                        g = t * 4 + h
                        act.activation(oo[:, g, :], pw[:, 2 + t, :], ACT.Copy).then_inc(sig("ro_saved"), 1)
                        act.activation(scr[:, 1536:2048], pw[:, 2 + t, :], ACT.Square, accum_out=sm[:, 136 + g:137 + g]).then_inc(sig("ro_copied"), 1)
                        w.more("ro_copied")
                    act.activation(sm[:, 144 + h:152:4], sm[:, 136 + h:144:4], ACT.Sqrt, scale=1.0 / 512,
                                   bias=eps_col(1.0)).then_inc(sig("act_result"), 1)
                for b in range(8):
                    w.more("ry", 2)
                    act.activation(ah[:, 2 * b:2 * b + 2, :].rearrange("p c t -> p (c t)"), go[:, b * 512:(b + 1) * 512], ACT.Copy).then_inc(sig("out_high"), 1)
                for j in range(4, 8):
                    split("b", o0 + j)
                ahead(UB[(1, "ffn2")], 2)
                residual_rms(o0 + 7, 1.0)

            for l in range(2):
                ffn(l, 1, 2 * l)
                (even, odd)[l]()
                ffn(l, 2, 2 * l + 1)
                ple(l)

        @block.vector
        def _(dve):
            w = Waits(dve)

            def then(ins, name="dve_step", n=1):
                ins.then_inc(sig(name), 1)
                w.more(name, n)

            def split(ep, u, it=0, per=0):
                dve.wait_ge(sig(f"{ep}_hi"), per * it + (u + 1))
                dve.tensor_tensor(wl[:, u % RING, :], raw[:, u % RING, :], wh[:, u % RING, :].bitcast(F32),
                                  ALU.subtract).then_inc(sig(f"{ep}_lo"), 1)

            def mean_square(eps=EPS):
                for t in range(NT):
                    dve.tensor_tensor_reduce(scr[:, t * D:(t + 1) * D], x[:, t, :], x[:, t, :], 1.0 / D, eps,
                                             ALU.mult, ALU.add, sm[:, 10 + t:11 + t]).then_inc(sig("dve_step"), 1)
                w.more("dve_step", 2)
                dve.sem_inc(sig("meansq_ready"), 1)

            def norm_in(col):
                mean_square()
                w.more("rms_ready")
                then(dve.reciprocal(sm[:, 14:16], sm[:, 12:14]))
                dve.sem_inc(sig("rstd_ready"), 1)
                dve.tensor_scalar(scr[:, 0:D], x[:, 0, :], sm[:, 14:15], None, ALU.mult).then_inc(sig("xn_ready"), 1)
                w.passed("xn_ready", 2)
                lows(col, KC)

            def lows(col, n, chunk=0):
                for c in range(n):
                    if c % 2 == 0:
                        w.more("high", 2)
                    src = pw[:, c // 2, (c % 2) * T:(c % 2 + 1) * T]
                    hi = rd[:, chunk + c, :]
                    if col is None:
                        ins = dve.tensor_tensor(al[:, chunk + c, :], src, hi, ALU.subtract)
                    else:
                        ins = dve.scalar_tensor_tensor(al[:, chunk + c, :], src, col(c), hi, ALU.mult, ALU.subtract)
                    ins.then_inc(sig("act_ready"), 1)

            dve.memset(sm[:, 168:169], EPS).then_inc(sig("dve_step"), 1)
            dve.memset(sm[:, 169:170], 4 * EPS).then_inc(sig("dve_step"), 1)
            w.more("dve_step", 2)
            w.more("x_loaded", 16)
            mean_square()
            w.more("rms_ready")
            then(dve.reciprocal(sm[:, 14:16], sm[:, 12:14]))
            dve.sem_inc(sig("rstd_ready"), 1)
            dve.tensor_scalar(scr[:, 0:D], x[:, 0, :], sm[:, 14:15], None, ALU.mult).then_inc(sig("xn_ready"), 1)
            w.passed("xn_ready", 2)
            w.more("vcol")
            lows(lambda c: vcol[:, 112 + c:113 + c], KC)

            def bias_rows():
                w.more("psum_for_dve")
                dve.tensor_copy(brow[0:NH, :], acc[0:NH, 3, 0:384]).then_inc(sig("bias_rows"), 1)

            def convolution():
                w.more("proj_evac", 2)
                for s in range(4):
                    for c in range(4):
                        src, dst = pF[:, F_C + c * T:F_C + (c + 1) * T], cact[:, c * T:(c + 1) * T]
                        tap = small_col(V_CW + (3 - s) * 4 + c)
                        if s == 0:
                            ins = dve.tensor_scalar(dst, src, tap, small_col(V_CB + c), ALU.mult, ALU.add)
                        else:
                            ins = dve.scalar_tensor_tensor(dst[:, s:T], src[:, 0:T - s], tap, dst[:, s:T], ALU.mult, ALU.add)
                        ins.then_inc(sig("dve_step"), 1)
                    w.more("dve_step", 4)
                dve.sem_inc(sig("dve_result"), 1)

            def lam():
                w.more("act_result")
                then(dve.tensor_tensor(sm[:, 92:93], sm[:, 90:91], sm[:, 91:92], ALU.subtract))
                then(dve.tensor_scalar(sm[:, 92:93], sm[:, 92:93], LAM0, None, ALU.add))
                then(dve.tensor_scalar(sm[:, 93:94], small_col(V_DA), 1.0 - LAM0, None, ALU.mult))
                dve.sem_inc(sig("lam"), 1)

            def gate_rows():
                w.more("psum_for_dve")
                f, g_abs, g_ln, g_i = (scr[0:NH, k:k + T] for k in (768, 1280, 1280, 1536))
                ones_row = scr[0:NH, 1792:2048]
                dve.memset(ones_row, 1.0).then_inc(sig("dve_step"), 1)
                then(dve.tensor_scalar(f, acc[0:NH, 0, T:2 * T], gbias[0:NH, 1:2], None, ALU.add), n=2)
                then(dve.tensor_scalar(g_abs, f, -1.0, None, ALU.mult))
                dve.tensor_tensor(g_abs, f, g_abs, ALU.max).then_inc(sig("dve_result"), 1)
                dve.tensor_scalar(g_i, acc[0:NH, 0, 0:T], gbias[0:NH, 0:1], None, ALU.add).then_inc(sig("dve_step"), 1)
                then(dve.tensor_scalar(f, f, 0.0, None, ALU.min), n=2)
                w.more("act_result")
                then(dve.tensor_tensor(f, f, g_ln, ALU.subtract))
                fsum = scr[0:NH, 1024:1280]
                then(dve.tensor_tensor_scan(fsum, ones_row, f, 0.0, ALU.mult, ALU.add))
                then(dve.tensor_tensor(a_row, g_i, fsum, ALU.subtract))
                then(dve.tensor_tensor_scan(mx_row, ones_row, a_row, 0.0, ALU.mult, ALU.max))
                then(dve.tensor_tensor(nm_row, fsum, mx_row, ALU.add))
                then(dve.tensor_scalar(nm_row, nm_row, -1.0, None, ALU.mult))
                dve.sem_inc(sig("gate_rows"), 1)

            for u in range(12):
                split("a", u)
                if u == 3:
                    w.more("mweights", 80)
                    dve.tensor_tensor(sm[0:64, 88:90], lamq[0:64, 0:4:2], lamq[0:64, 1:4:2], ALU.mult).then_inc(sig("lam_prod"), 1)
                if u == 5:
                    bias_rows()
                    convolution()
                if u == 8:
                    w.more("qk_psum")
                    dve.tensor_copy(km.rearrange("p (b n) -> p b n", b=2), acc[:, 2:4, :]).then_inc(sig("km"), 1)
                    dve.memset(vt1[:, :, :, P:P + 1], 1.0).then_inc(sig("vt1"), 1)
                if u == 9:
                    lam()
            gate_rows()
            split("a", 12)
            split("a", 13)
            w.more("proj_evac", 10)
            w.more("psum_for_dve")
            dve.tensor_copy(sm[:, 16:32], acc[:, 1, 0:16]).then_inc(sig("gate_cols"), 1)
            w.more("gate_cols")

            def exponents(h):
                e = scr[:, 768 + 384 * (h % 2):768 + 384 * (h % 2 + 1)]
                mrow = acc[:, 2 + h // 2, (h % 2) * T:(h % 2 + 1) * T]
                dve.tensor_scalar(e[:, 0:T], mrow, sm[:, 16 + h:17 + h], 0.0, ALU.subtract, ALU.max).then_inc(sig("dve_step"), 1)
                then(dve.tensor_scalar(e[:, T:T + P], mrow[:, P:T], sm[:, 20 + h:21 + h], 0.0, ALU.subtract, ALU.max), n=2)
                dve.sem_inc(sig("exponents_ready"), 1)
                return e

            exponents(0)
            for h in range(NH):
                if h + 1 < NH:
                    exponents(h + 1)
                e = scr[:, 768 + 384 * (h % 2):768 + 384 * (h % 2 + 1)]
                w.more("exponentials")
                then(dve.tensor_tensor(e, e, cst("mask3"), ALU.mult))
                w.more("pairs_ready")
                if h >= 2:
                    w.more("heads_ready")
                dve.scalar_tensor_tensor(mw[h % 2], pw[:, h % 2, 0:384], P ** -0.5, e, ALU.mult, ALU.mult).then_inc(sig("dve_step"), 1)
                w.more("dve_step")
                dve.sem_inc(sig("weights_ready"), 1)
                dve.sem_inc(sig("pairs_used"), 1)
            for h in range(NH):
                dve.tensor_scalar(arena[:, F_C + h * T:F_C + (h + 1) * T], cact[:, h * T:(h + 1) * T], small_col(V_SK + h), None,
                                  ALU.mult).then_inc(sig("dve_step"), 1)
            w.more("dve_step", 4)
            split("a", 14)
            w.more("heads_ready", 2)
            w.more("heads_copied", 4)
            w.more("floor")
            den = sm[:, 32:40]
            obf = ob.rearrange("p t h d -> p (t h) d")

            def bc(col):
                return col.unsqueeze(2).broadcast_to([P, 8, P])

            then(dve.tensor_scalar(sm[:, 40:48], den, -1.0, None, ALU.mult))
            then(dve.tensor_tensor(den, den, sm[:, 40:48], ALU.max))
            then(dve.tensor_tensor(den, den, sm[:, 24:32], ALU.max))
            then(dve.reciprocal(sm[:, 48:56], den))
            then(dve.tensor_tensor(obf, obf, bc(sm[:, 48:56]), ALU.mult))
            then(dve.reduce_sum(sm[:, 56:64], obf, AX))
            then(dve.tensor_scalar(sm[:, 56:64], sm[:, 56:64], 1.0 / P, None, ALU.mult))
            then(dve.tensor_tensor(obf, obf, bc(sm[:, 56:64]), ALU.subtract))

            def head_rstd(src, eps):
                sq = scr[:, 0:1024].rearrange("p (g d) -> p g d", g=8)
                then(dve.tensor_tensor(sq, src, src, ALU.mult))
                then(dve.reduce_sum(sm[:, 64:72], sq, AX))
                dve.tensor_scalar(sm[:, 64:72], sm[:, 64:72], 1.0 / P, eps, ALU.mult, ALU.add).then_inc(sig("dve_result"), 1)
                w.more("act_result")
                then(dve.reciprocal(sm[:, 80:88], sm[:, 72:80]))
                dve.tensor_tensor(src, src, bc(sm[:, 80:88]), ALU.mult).then_inc(sig("heads_normed"), 1)

            head_rstd(obf, EPS)
            w.more("heads_turned")
            for h in range(NH):
                y = arena[:, F_C + h * T:F_C + (h + 1) * T]
                src = acc[:, h // 2, (h % 2) * T:(h % 2 + 1) * T]
                then(dve.scalar_tensor_tensor(y, src, small_col(V_MG + h), y, ALU.mult, ALU.add))
                then(dve.tensor_tensor(y, y, pF[:, F_Z + h * T:F_Z + (h + 1) * T], ALU.mult), "head_gated")
            for h in range(NH):
                w.more("high")
                dve.tensor_tensor(al[:, h, :], arena[:, F_C + h * T:F_C + (h + 1) * T], rd[:, h, :], ALU.subtract).then_inc(sig("act_ready"), 1)
            w.more("btile", 16)

            def diff_soft(h):
                b = pw[:, 2 * (h % 2):2 * (h % 2) + 2, :]
                k = 96 + 4 * (h % 2)
                lo = dlog[h % 2]
                w.more("pairs_ready")
                for t, (c0, n) in enumerate(((0, P), (P, T))):
                    bias = btile[:, h, T - n:T].unsqueeze(1).broadcast_to([P, 2, n])
                    dve.scalar_tensor_tensor(lo[:, :, c0:c0 + n], b[:, :, c0:c0 + n], 64 ** -0.5, bias, ALU.mult, ALU.add).then_inc(sig("dve_step"), 1)
                w.more("dve_step", 2)
                dve.sem_inc(sig("pairs_used"), 1)
                for t, (c0, n) in enumerate(((0, P), (P, T))):
                    dve.tensor_reduce(sm[:, k + 2 * t:k + 2 * t + 2], lo[:, :, c0:c0 + n], AX, ALU.max, negate=True).then_inc(sig("exponents_ready"), 1)
                w.passed("exponents_ready", 2)

            diff_soft(0)
            for h in range(NH):
                if h + 1 < NH:
                    diff_soft(h + 1)
                k = 96 + 4 * (h % 2)
                lo = dlog[h % 2]
                w.more("exponentials", 4)
                then(dve.reciprocal(sm[:, 112:116], sm[:, k + 8:k + 12]))
                then(dve.tensor_scalar(sm[:, 113:116:2], sm[:, 113:116:2], sm[:, 92:93], None, ALU.mult))
                for t, (c0, n) in enumerate(((0, P), (P, T))):
                    dve.tensor_scalar(lo[:, 1, c0:c0 + n], lo[:, 1, c0:c0 + n], sm[:, 113 + 2 * t:114 + 2 * t], None, ALU.mult).then_inc(sig("dve_step"), 1)
                w.more("dve_step", 2)
                if h >= 1:
                    w.more("weights_turned_psum")
                for t, (c0, n) in enumerate(((0, P), (P, T))):
                    dve.scalar_tensor_tensor(dmix[:, c0:c0 + n], lo[:, 0, c0:c0 + n], sm[:, 112 + 2 * t:113 + 2 * t],
                                             lo[:, 1, c0:c0 + n], ALU.mult, ALU.subtract).then_inc(sig("dve_step"), 1)
                w.more("dve_step", 2)
                dve.sem_inc(sig("weights_ready"), 1)
            dve.sem_inc(sig("btile_used"), 1)
            w.passed("weights_turned_psum", 1)
            w.passed("heads_ready", 4)
            w.more("heads_copied", 4)
            obf2 = ob2.rearrange("p t h d -> p (t h) d")
            head_rstd(obf2, SUBLN_EPS)
            w.more("heads_turned")
            for h in range(NH):
                if h % 2 == 0:
                    w.more("high", 2)
                dve.scalar_tensor_tensor(al[:, 4 + h, :], pw[:, h // 2, (h % 2) * T:(h % 2 + 1) * T], sm[:, 93:94],
                                         rd[:, 4 + h, :], ALU.mult, ALU.subtract).then_inc(sig("act_ready"), 1)
            split("a", 15)
            dve.memset(zr[:, :].bitcast(F32), 0.0).then_inc(sig("zr"), 1)
            dve.memset(selT.bitcast(F32), 0.0).then_inc(sig("selT_ready"), 1)
            dve.memset(slot_gate, 0.0).then_inc(sig("selT_ready"), 1)
            dve.memset(rt[:, 72:84], 0.0).then_inc(sig("dve_step"), 1)
            dve.memset(pos_all, 0.0).then_inc(sig("dve_step"), 1)
            dve.memset(gate_all, 0.0).then_inc(sig("dve_step"), 1)
            w.more("dve_step", 3)
            dve.wait_ge(sig("a_used"), NA + RING)
            for t in range(NT):
                xt = x[:, t, :].rearrange("p (b n) -> p b n", b=2)
                dve.tensor_tensor(xt, xt, acc[:, 2 * t:2 * t + 2, :], ALU.add).then_inc(sig("x_new"), 1)
            w.more("x_new", 2)
            w.more("rms_ready")
            then(dve.reciprocal(sm[:, 14:16], sm[:, 12:14]))
            w.more("gain_loaded", 16)
            for t in range(NT):
                dve.scalar_tensor_tensor(h2[:, t, :], x[:, t, :], sm[:, 14 + t:15 + t], gb[:, :], ALU.mult, ALU.mult).then_inc(sig("h2_ready"), 1)
            w.more("h2_ready", 2)
            dve.sem_inc(sig("gain_free"), 1)
            for t in range(NT):
                w.more("h2_high")
                src = h2[:, t, :].rearrange("p (f k) -> p k f", k=KC)
                hi = h2h[:, t, :, :]
                dve.tensor_tensor(h2l[:, t, :, :], src, hi.bitcast(F32), ALU.subtract).then_inc(sig("h2_split"), 1)
            split("m", 0)
            split("m", 1)
            w.more("psum_for_dve")
            w.more("router", 64)
            lr = rt[:, 0:72].rearrange("p (t n) -> p t n", t=NT)
            for t in range(NT):
                dve.tensor_tensor(lr[:, t, :], acc[:, 0, t * 36:(t + 1) * 36], br, ALU.add).then_inc(sig("dve_step"), 1)
            w.more("dve_step", 2)

            def r3(c0, n):
                return rt[:, c0:c0 + NT * n].rearrange("p (t n) -> p t n", t=NT)

            def wide(col, n):
                return col.unsqueeze(2).broadcast_to([P, NT, n])

            def first_max(src, n, top, hot, tie):
                then(dve.tensor_reduce(top, src, AX, ALU.max))
                then(dve.tensor_tensor(hot, src, wide(top, n), ALU.is_equal))
                then(dve.tensor_tensor(hot, hot, tie.unsqueeze(1).broadcast_to([P, NT, n]), ALU.mult))
                then(dve.tensor_reduce(rt[:, 84:86], hot, AX, ALU.max))
                then(dve.tensor_tensor(hot, hot, wide(rt[:, 84:86], n), ALU.is_equal))

            tie4, tie8 = cst("tie")[:, 0:4], cst("tie")[:, 4:12]
            lg, le = lr[:, :, 0:4], lr[:, :, 4:36]
            gtop, ghot = rt[:, 86:88], r3(88, 4)
            first_max(lg, 4, gtop, ghot, tie4)
            then(dve.tensor_tensor(r3(72, 4), lg, wide(gtop, 4), ALU.subtract))
            dve.sem_inc(sig("dve_result"), 1)
            prod = rt[:, 96:160]
            for t in range(NT):
                dve.tensor_tensor(prod[:, t * 32:(t + 1) * 32].rearrange("p (g j) -> p g j", g=4), le[:, t, :].rearrange("p (g j) -> p g j", g=4),
                                  ghot[:, t, :].unsqueeze(2).broadcast_to([P, 4, 8]), ALU.mult).then_inc(sig("dve_step"), 1)
            w.more("dve_step", 2)
            sel8 = r3(160, 8)
            then(dve.reduce_sum(sel8, prod.rearrange("p (t g j) -> p t j g", t=NT, g=4), AX))
            hot1, hot2, rest = r3(176, 8), r3(192, 8), r3(208, 8)
            top1, top2 = rt[:, 224:226], rt[:, 226:228]
            first_max(sel8, 8, top1, hot1, tie8)
            then(dve.scalar_tensor_tensor(rest, hot1, NEG, sel8, ALU.mult, ALU.add))
            first_max(rest, 8, top2, hot2, tie8)
            then(dve.tensor_tensor(rt[:, 82:84], top2, top1, ALU.subtract))
            dve.sem_inc(sig("dve_result"), 1)
            w.more("act_result", 2)
            then(dve.reduce_sum(rt[:, 228:230], r3(72, 4), AX))
            then(dve.reciprocal(rt[:, 228:230], rt[:, 228:230]))
            then(dve.tensor_scalar(rt[:, 230:232], rt[:, 82:84], 1.0, None, ALU.add))
            then(dve.reciprocal(rt[:, 230:232], rt[:, 230:232]))
            then(dve.tensor_tensor(rt[:, 230:232], rt[:, 230:232], rt[:, 228:230], ALU.mult))
            then(dve.tensor_tensor(rt[:, 232:234], rt[:, 230:232], rt[:, 82:84], ALU.mult))
            both = r3(240, 8)
            then(dve.tensor_tensor(both, hot1, hot2, ALU.add))
            then(dve.tensor_tensor(hot1, hot1, wide(rt[:, 230:232], 8), ALU.mult))
            then(dve.tensor_tensor(hot2, hot2, wide(rt[:, 232:234], 8), ALU.mult))
            then(dve.tensor_tensor(hot1, hot1, hot2, ALU.add))
            for t in range(NT):
                g4 = ghot[:, t, :].unsqueeze(2).broadcast_to([P, 4, 8])
                for val, dst in ((both, masks), (hot1, gate_all)):
                    dve.tensor_tensor(dst[:, t, 0:32].rearrange("p (g j) -> p g j", g=4), g4,
                                      val[:, t, :].unsqueeze(1).broadcast_to([P, 4, 8]), ALU.mult).then_inc(sig("dve_step"), 1)
            w.more("dve_step", 4)
            dve.sem_inc(sig("masks"), 1)
            w.more("psum_for_dve")
            for t in range(NT):
                dve.scalar_tensor_tensor(pos_all[:, t, 0:32], masks[:, t, :], -BIG, acc[:, 1, t * 32:(t + 1) * 32], ALU.mult, ALU.add).then_inc(sig("dve_step"), 1)
            then(dve.tensor_reduce(rt[:, 256:257], acc[:, 1, 64:96], AX, ALU.max), n=3)
            dve.sem_inc(sig("positions_read"), 1)
            for r in range(1, ROUNDS):
                dve.tensor_scalar(pos_all[:, :, r * 32:(r + 1) * 32], pos_all[:, :, 0:32], -float(r * CAP), None, ALU.add).then_inc(sig("dve_step"), 1)
                dve.tensor_copy(gate_all[:, :, r * 32:(r + 1) * 32], gate_all[:, :, 0:32]).then_inc(sig("dve_step"), 1)
                dve.tensor_scalar(rt[:, 256 + r:257 + r], rt[:, 256:257], r * CAP + 0.5, None, ALU.is_gt).then_inc(sig("dve_step"), 1)
            w.more("dve_step", 3 * (ROUNDS - 1))
            dve.sem_inc(sig("positions_ready"), 1)
            then(dve.reduce_sum(rt[:, 260:261], rt[:, 257:256 + ROUNDS], AX))
            then(dve.tensor_copy(nrounds_i[0:1, 0:1], rt[0:1, 260:261]))
            dve.sem_inc(sig("rounds_ready"), 1)
            dve.wait_ge(sig("gathered"), 1)
            dve.tensor_copy(xg[:, 4:8, :], pw[:, 1, :].rearrange("p (k s) -> p k s", k=4)).then_inc(sig("xg_ready"), 1)
            nr = dve.value_load(nrounds_i[0:1, 0:1], min_val=0, max_val=ROUNDS - 1)

            def lower_output(i):
                dve.wait_ge(sig("yd_high"), i + 1)
                dve.wait_ge(sig("selT_ready"), i * 2 + 2)
                dve.scalar_tensor_tensor(ydl.rearrange("p (b n) -> p b n", b=2), pw[:, 0:2, :], slot_gate,
                                         ydh.bitcast(F32).rearrange("p (b n) -> p b n", b=2), ALU.mult, ALU.subtract).then_inc(sig("yd_ready"), 1)

            with dve.Fori(0, nr * E + E) as i:
                for j in range(2, 6):
                    split("m", j, i, 6)
                    if j == 3:
                        lower_output(i)
                dve.wait_ge(sig("silu"), i + 1)
                dve.tensor_tensor(hid_s, silu_s, pw[:, 2, 256:512], ALU.mult).then_inc(sig("hid_s"), 1)
                dve.wait_ge(sig("hid_high"), i + 1)
                dve.tensor_tensor(hid[:, :, CAP:P], hid_s.rearrange("p (c s) -> p c s", c=4), hid[:, :, 0:CAP].bitcast(F32),
                                  ALU.subtract).then_inc(sig("hid_ready"), 1)
                dve.wait_ge(sig("gathered"), i + 2)
                dve.tensor_copy(xg[:, 4:8, :], pw[:, 1, :].rearrange("p (k s) -> p k s", k=4)).then_inc(sig("xg_ready"), 1)
                split("m", 6, i, 6)
                dve.wait_ge(sig("selT_done"), i + 2)
                dve.wait_ge(sig("scattered"), i + 1)
                dve.tensor_scalar(selT, pw[:, 3, 0:T], 0.0, None, ALU.is_gt).then_inc(sig("selT_ready"), 1)
                dve.tensor_reduce(slot_gate, pw[:, 3, 0:T], AX, ALU.max).then_inc(sig("selT_ready"), 1)
                split("m", 7, i, 6)
            total = nr * E + E
            lower_output(total)
            dve.wait_ge(sig("m_lo"), total * 6 + 2)
            dve.sem_inc(sig("b_lo"), 2)
            dve.wait_ge(sig("scattered"), total + 1)
            for t in range(NT):
                dve.tensor_tensor(x[:, t, :].rearrange("p (b n) -> p b n", b=2), x[:, t, :].rearrange("p (b n) -> p b n", b=2),
                                  acc[:, 2 * t:2 * t + 2, :], ALU.add).then_inc(sig("dve_step"), 1)
            w.more("dve_step", 2)
            mean_square()
            w.more("rms_ready")
            then(dve.reciprocal(sm[:, 14:16], sm[:, 12:14]))
            w.more("gain_loaded", 16)
            for t in range(NT):
                dve.scalar_tensor_tensor(x[:, t, :], x[:, t, :], sm[:, 14 + t:15 + t], gb[:, :], ALU.mult, ALU.mult).then_inc(sig("x_new"), 1)
            w.more("x_new", 2)
            dve.sem_inc(sig("gain_free"), 1)

            w.more("consts", 48)

            def ahead(u, n):
                for j in range(n):
                    split("b", u + j)

            def norm_in(col, late=None):
                for t in range(NT):
                    w.more("rms_ready")
                    then(dve.reciprocal(sm[:, 14 + t:15 + t], sm[:, 12 + t:13 + t]))
                    dve.tensor_scalar(diag[:, t, :], ident, sm[:, 14 + t:15 + t], None, ALU.mult).then_inc(sig("diag_ready"), 1)
                if late is not None:
                    split("b", late)
                lows(col, KC)

            def add_normed(src, u, product=None):
                w.more("gain_loaded", 16)
                g2 = gb[:, :].rearrange("p (b n) -> p b n", b=2)
                for t in range(NT):
                    if u is None:
                        product(t)
                    w.more("squares")
                    then(dve.tensor_tensor(scr[:, t * D:(t + 1) * D].rearrange("p (b n) -> p b n", b=2), src(t), g2, ALU.mult))
                    if t == 1:
                        dve.sem_inc(sig("gain_free"), 1)
                    w.more("rms_ready")
                    then(dve.reciprocal(sm[:, 14 + t:15 + t], sm[:, 12 + t:13 + t]))
                    dve.scalar_tensor_tensor(x[:, t, :], scr[:, t * D:(t + 1) * D], sm[:, 14 + t:15 + t], x[:, t, :],
                                             ALU.mult, ALU.add).then_inc(sig("x_new"), 1)
                w.more("x_new", 2)

            def in_psum(t):
                return acc[:, 2 * t:2 * t + 2, :]

            def ffn(l, n, idx):
                u0, done = UB[(l, f"ffn{n}")], idx * FB
                norm_in(lambda c: norm_col(l, 4 * (n - 1), c), u0 + 1 if l == 1 and n == 1 else None)

                def activate(par, it, b):
                    hb = scr[:, 1024 + par * 512:1536 + par * 512]
                    dve.wait_ge(sig("ff_silu"), it * 2 + (done + b + 1))
                    dve.tensor_tensor(hb, scr[:, par * 512:(par + 1) * 512], pw[:, 2 * par + 1, :], ALU.mult).then_inc(sig("ff_hid"), 1)
                    dve.wait_ge(sig("ff_high"), it * 2 + (done + b + 1))
                    dve.tensor_tensor(al[:, 8 + 2 * par:10 + 2 * par, :].rearrange("p c t -> p (c t)"), hb,
                                      rd[:, 8 + 2 * par:10 + 2 * par, :].rearrange("p c t -> p (c t)"), ALU.subtract).then_inc(sig("ff_ready"), 1)

                with dve.Fori(0, 5) as it:
                    for par in range(2):
                        u = u0 + 2 + 3 * par
                        split("b", u, it, 6)
                        split("b", u + 1, it, 6)
                        activate(par, it, par)
                        split("b", u + 2, it, 6)
                split("b", u0 + 32)
                activate(0, 0, FB - 1)
                ahead(u0 + 33, 2)
                add_normed(in_psum, u0 + 32)

            def ple(l):
                dve.sem_inc(sig("x_ready"), 1)
                split("b", UB[(l, "ple_gate")] + 2)
                lows(None, KC)
                w.more("high")
                dve.tensor_tensor(al[:, 8:10, :].rearrange("p c t -> p (c t)"), acc[:, 0, :],
                                  rd[:, 8:10, :].rearrange("p c t -> p (c t)"), ALU.subtract).then_inc(sig("act_ready"), 1)
                u0 = UB[(l, "ple_gate")]
                split("b", u0 + 3)
                split("b", u0 + 4)
                if l == 0:
                    ahead(u0 + 5, 1)

                def product(t):
                    if t == 0:
                        dve.wait_ge(sig("first_tile"), 4 * l + 4)
                    else:
                        dve.wait_ge(sig("b_used"), u0 + 5 + RING)
                    y = sg[:, t, :].rearrange("p (b n) -> p b n", b=2)
                    then(dve.tensor_tensor(y, acc[:, 2 * t:2 * t + 2, :], y, ALU.mult))
                    dve.sem_inc(sig("ple_y"), 1)

                add_normed(lambda t: sg[:, t, :].rearrange("p (b n) -> p b n", b=2), None, product)

            def trig(l, freq):
                pos, k, cos, sin = rope[l]
                ang = trig_in[l]
                w.more("pos", 32)
                then(dve.tensor_copy(ang, pos.bitcast(I32)))
                then(dve.tensor_scalar(ang, ang, freq, None, ALU.mult))
                magic = 12582912.0
                then(dve.tensor_scalar(k, ang, 1.0 / TWO_PI, magic, ALU.mult, ALU.add))
                then(dve.tensor_scalar(k, k, magic, None, ALU.subtract))
                c1 = 6.28125
                c2 = float(np.round((TWO_PI - c1) * 2 ** 20) / 2 ** 20)
                for c in (c1, c2, TWO_PI - c1 - c2):
                    then(dve.scalar_tensor_tensor(ang, k, -c, ang, ALU.mult, ALU.add))
                then(dve.tensor_scalar(ang, ang, 3.1415925, -3.1415925, ALU.min, ALU.max))
                dve.sem_inc(sig("dve_result"), 1)
                w.more("act_result", 2)
                then(dve.tensor_tensor(cos, cos, cos, ALU.mult))
                then(dve.tensor_scalar(cos, cos, -2.0, 1.0, ALU.mult, ALU.add))

            def even():
                u0 = UB[(0, "mix_in")]
                norm_in(lambda c: norm_col(0, 2, c), u0 + 2)
                dve.sem_inc(sig("pos_space"), 1)
                trig(0, cst("freq_b"))
                dve.tensor_tensor(sm[:, 120:124], vcol[:, P + V_LB:P + V_LB + 4], vcol[:, P + V_LB + 4:P + V_LB + 8], ALU.subtract).then_inc(sig("dve_result"), 1)
                w.more("act_result")
                then(dve.tensor_scalar(sm[:, 128:132], sm[:, 124:128], -1.0, 1.0, ALU.mult, ALU.add))
                def log_sums():
                    w.more("act_result")
                    dve.tensor_scalar(fk, fk, -1.0, 1.0, ALU.mult, ALU.add).then_inc(sig("dve_step"), 1)
                    for g in range(16):
                        dve.tensor_tensor_scan(bsum[:, g * 64:(g + 1) * 64], cst("mask3")[:, P:P + 64], kd[:, g * 64:(g + 1) * 64],
                                               0.0, ALU.mult, ALU.add).then_inc(sig("dve_step"), 1)
                    w.more("dve_step", 17)
                    dve.sem_inc(sig("dve_result"), 1)
                    b16 = bsum.rearrange("p (g c) -> p g c", c=64)
                    kd16 = kd.rearrange("p (g c) -> p g c", c=64)
                    dve.tensor_tensor(kd16, b16[:, :, 63:64].broadcast_to([P, 16, 64]), b16, ALU.subtract).then_inc(sig("dve_result"), 1)

                def decayed():
                    w.more("act_result", 4)
                    dve.tensor_tensor(qs, qs, eb, ALU.mult).then_inc(sig("dve_step"), 1)
                    dve.tensor_tensor(ks, ks, fk, ALU.mult).then_inc(sig("dve_step"), 1)
                    dve.tensor_tensor(kd, kd, fk, ALU.mult).then_inc(sig("dve_step"), 1)
                    w.more("dve_step", 3)
                    dec = sm[:, 136:152].rearrange("p (h n) -> p h n", n=4)
                    kd4 = kd.rearrange("p (h n c) -> p h n c", n=4, c=64)
                    far = [eb[:, v * T:(v + 1) * T].rearrange("p (h c) -> p h c", h=NH) for v in range(3)]

                    def by(n):
                        return dec[:, :, n:n + 1].broadcast_to([P, NH, 64])

                    dve.tensor_tensor(far[2], kd4[:, :, 1, :], by(2), ALU.mult).then_inc(sig("dve_step"), 1)
                    dve.tensor_tensor(far[0], kd4[:, :, 0, :], by(1), ALU.mult).then_inc(sig("dve_step"), 1)
                    w.more("dve_step", 2)
                    then(dve.tensor_tensor(far[1], far[0], by(2), ALU.mult))
                    dve.sem_inc(sig("hgrn_ready"), 1)

                for j in range(3, 11):
                    split("b", u0 + j)
                    if j == 6:
                        w.more("proj_evac", 4)
                        for h in range(NH):
                            f = fk[:, h * T:(h + 1) * T]
                            dve.tensor_scalar(f, f, sm[:, 128 + h:129 + h], sm[:, 124 + h:125 + h], ALU.mult, ALU.add).then_inc(sig("dve_step"), 1)
                        w.more("dve_step", 4)
                        dve.sem_inc(sig("dve_result"), 1)
                    if j == 7:
                        log_sums()
                    if j == 9:
                        decayed()
                w.more("proj_evac", 7)
                w.more("psum_for_dve")
                _, _, cos, sin = rope[0]

                def over(a, n):
                    return a.unsqueeze(1).broadcast_to([P, n, T])

                def v4(a, n):
                    return a.rearrange("p (c t) -> p c t", c=n)

                q_psum = acc[:, 0:2, :].rearrange("p b (c t) -> p (b c) t", c=2)
                tmp = scr[:, 0:1024]
                dve.tensor_tensor(v4(tmp, 4), q_psum, over(sin, 4), ALU.mult).then_inc(sig("dve_step"), 1)
                dve.tensor_tensor(v4(qr, 4), v4(qb, 4), over(cos, 4), ALU.mult).then_inc(sig("dve_step"), 1)
                dve.tensor_tensor(v4(kr, 2), v4(acc[:, 2, :], 2), over(cos, 2), ALU.mult).then_inc(sig("dve_step"), 1)
                dve.tensor_tensor(v4(scr[:, 1024:1536], 2), v4(acc[:, 3, :], 2), over(sin, 2), ALU.mult).then_inc(sig("dve_step"), 1)
                w.more("dve_step", 4)
                dve.tensor_tensor(qr, qr, tmp, ALU.add).then_inc(sig("dve_step"), 1)
                dve.tensor_tensor(kr, kr, scr[:, 1024:1536], ALU.add).then_inc(sig("dve_step"), 1)
                w.more("dve_step", 2)
                dve.sem_inc(sig("roped"), 1)

                def soft(h):
                    k = 96 + 8 * (h % 2)
                    w.more("pairs_ready")
                    lo = swl[h % 2]
                    if h >= 2:
                        w.more("weights_turned_psum")
                    then(dve.scalar_tensor_tensor(lo, pw[:, h % 2, 0:384], 64 ** -0.5, cst("band3"), ALU.mult, ALU.add))
                    dve.sem_inc(sig("pairs_used"), 1)
                    for t, (c0, n) in enumerate(((0, P), (P, T))):
                        dve.reduce_max(sm[:, k + t:k + t + 1], lo[:, c0:c0 + n], AX).then_inc(sig("dve_step"), 1)
                    w.more("dve_step", 2)
                    dve.tensor_scalar(sm[:, k:k + 2], sm[:, k:k + 2], sinks[:, h:h + 1], -1.0, ALU.max, ALU.mult).then_inc(sig("exponents_ready"), 1)

                soft(0)
                for h in range(8):
                    if h + 1 < 8:
                        soft(h + 1)
                    k = 96 + 8 * (h % 2)
                    w.more("exponentials", 3)
                    then(dve.tensor_tensor(sm[:, k + 2:k + 4], sm[:, k + 2:k + 4], sm[:, k + 4:k + 6], ALU.add))
                    then(dve.reciprocal(sm[:, k + 6:k + 8], sm[:, k + 2:k + 4]))
                    for t, (c0, n) in enumerate(((0, P), (P, T))):
                        e = swl[h % 2][:, c0:c0 + n]
                        dve.tensor_scalar(e, e, sm[:, k + 6 + t:k + 7 + t], None, ALU.mult).then_inc(sig("dve_step"), 1)
                    w.more("dve_step", 2)
                    dve.sem_inc(sig("weights_ready"), 1)
                    if h < 4:
                        split("b", UB[(0, "mix_out")] + h)
                w.more("weights_turned_psum", 2)
                w.more("high", 2)
                for b in range(2):
                    dve.tensor_tensor(al[:, 4 + 2 * b:6 + 2 * b, :].rearrange("p c t -> p (c t)"), pw[:, 2 + b, :],
                                      rd[:, 4 + 2 * b:6 + 2 * b, :].rearrange("p c t -> p (c t)"), ALU.subtract).then_inc(sig("act_ready"), 1)
                for h in range(NH):
                    w.more("pairs_ready")
                    if h >= 2:
                        w.more("heads_ready")
                    then(dve.tensor_tensor(swl[h % 2], pw[:, h % 2, 0:384], cst("mask3"), ALU.mult))
                    dve.sem_inc(sig("pairs_used"), 1)
                    dve.sem_inc(sig("weights_ready"), 1)
                w.more("heads_ready", 2)
                w.more("heads_copied", 4)
                head_rstd(oh.rearrange("p t h d -> p (t h) d"), EPS)
                w.more("heads_turned")
                for h in range(NH):
                    g = ga[:, h * T:(h + 1) * T]
                    dve.scalar_tensor_tensor(g, pw[:, h // 2, (h % 2) * T:(h % 2 + 1) * T], small_col(V_HG), g, ALU.mult, ALU.mult).then_inc(sig("head_gated"), 1)
                for h in range(NH):
                    w.more("high")
                    dve.tensor_tensor(al[:, h, :], ga[:, h * T:(h + 1) * T], rd[:, h, :], ALU.subtract).then_inc(sig("act_ready"), 1)
                ahead(UB[(0, "ffn2")], 2)
                add_normed(in_psum, UB[(0, "mix_out")] + 3)

            def odd():
                u0 = UB[(1, "mix_in")]
                norm_in(lambda c: norm_col(1, 2, c), u0 + 2)
                dve.sem_inc(sig("pos_space"), 1)
                trig(1, cst("freq_c"))
                _, _, cos, sin = rope[1]

                def turn(c):
                    x1, x2 = (arena[:, (2 * c + k) * T:(2 * c + k + 1) * T] for k in range(2))
                    t1, t2 = scr[:, 512:768], scr[:, 768:1024]
                    dve.tensor_tensor(t1, x2, sin, ALU.mult).then_inc(sig("dve_step"), 1)
                    dve.tensor_tensor(t2, x1, sin, ALU.mult).then_inc(sig("dve_step"), 1)
                    w.more("dve_step", 2)
                    dve.tensor_tensor(x1, x1, cos, ALU.mult).then_inc(sig("dve_step"), 1)
                    dve.tensor_tensor(x2, x2, cos, ALU.mult).then_inc(sig("dve_step"), 1)
                    w.more("dve_step", 2)
                    dve.tensor_tensor(x1, x1, t1, ALU.subtract).then_inc(sig("dve_step"), 1)
                    dve.tensor_tensor(x2, x2, t2, ALU.add).then_inc(sig("dve_step"), 1)
                    w.more("dve_step", 2)

                for j in range(3, 24):
                    split("b", u0 + j)
                    if j == 13:
                        w.more("proj_evac", 8)
                    if 13 <= j < 21:
                        turn(j - 13)
                dve.sem_inc(sig("roped"), 1)
                o0 = UB[(1, "mix_out")]
                w.more("proj_evac", 16)

                def decayed(h):
                    w.more("pairs_ready")
                    if h >= 2:
                        w.more("heads_ready")
                    dec = cB[:, h * T:(h + 1) * T]
                    wt = ratt[h % 2]
                    dve.tensor_tensor(wt[:, 0:T], pw[:, h % 2, 0:T], dec, ALU.mult).then_inc(sig("dve_step"), 1)
                    dve.tensor_tensor(wt[:, T:T + P], pw[:, h % 2, T:T + P], dec[:, 0:P], ALU.mult).then_inc(sig("dve_step"), 1)
                    w.more("dve_step", 2)
                    dve.sem_inc(sig("pairs_used"), 1)
                    dve.sem_inc(sig("weights_ready"), 1)

                def normed(h):
                    w.more("act_result")
                    r = sm[:, 144 + h:152:4]
                    then(dve.reciprocal(r, r))
                    o = oo.rearrange("p (t h) d -> p t h d", t=NT)[:, :, h, :]
                    dve.tensor_tensor(o, o, r.unsqueeze(2).broadcast_to([P, NT, 512]), ALU.mult).then_inc(sig("heads_normed"), 1)

                decayed(0)
                for h in range(NH):
                    if h + 1 < NH:
                        decayed(h + 1)
                    split("b", o0 + h)
                    normed(h)
                w.more("heads_ready", 2)

                for b in range(8):
                    w.more("ro_turned")
                    for c in (2 * b, 2 * b + 1):
                        g = go[:, c * T:(c + 1) * T]
                        dve.scalar_tensor_tensor(g, pw[:, b % 4, (c % 2) * T:(c % 2 + 1) * T], small_col(V_RG + c % 4), g,
                                                 ALU.mult, ALU.mult).then_inc(sig("ry"), 1)
                for j in range(4, 8):
                    split("b", o0 + j)
                ahead(UB[(1, "ffn2")], 2)
                add_normed(in_psum, o0 + 7)

            for l in range(2):
                ffn(l, 1, 2 * l)
                (even, odd)[l]()
                ffn(l, 2, 2 * l + 1)
                ple(l)
            dve.sem_inc(sig("out_ready"), 1)


INPUTS = ["x", "w_in", "conv_w", "conv_b", "w_mq", "w_mk", "w_mgate", "b_mgate", "m_norm_g", "m_skip", "lambda_qk",
          "da_norm_g", "rel_bias", "w_out", "norm1_g", "norm2_g", "w_rg", "b_rg", "w_re", "b_re", "w_eg", "w_eu", "w_ed",
          "normf_g", "p_2", "positions_2", "norm_g_2", "ffn1_w_in_2", "ffn1_w_out_2", "ffn2_w_in_2", "ffn2_w_out_2",
          "ple_w_proj_2", "ple_w_gate_2", "even_w_in_2", "even_w_out_2", "hgrn_lb_2", "hgrn_onorm_g_2", "attn_sinks_2",
          "odd_w_in_2", "odd_w_out_2", "ret_onorm_g_2"]


def kernel(**inputs):
    import concourse.bacc as bacc
    from concourse.bass_utils import run_bass_kernel_spmd
    nc = bacc.Bacc("TRN2", target_bir_lowering=False, num_devices=1)
    arrays, aps = {}, {}
    given = {name: inputs[name] for name in INPUTS}
    given |= {"consts_always": ALWAYS, "consts_first": FIRST, "consts_second": SECOND, "decays": DECAYS}
    for name, value in given.items():
        v = np.ascontiguousarray(value)
        arrays[f"in_{name}"] = v
        aps[name] = nc.dram_tensor(f"in_{name}", v.shape, mybir.dt.from_np(v.dtype), kind="ExternalInput").ap()
    out = nc.dram_tensor("out", (1, T, D), F32, kind="ExternalOutput").ap()
    two_block_kernel(nc, aps, out)
    return run_bass_kernel_spmd(nc, [arrays], core_ids=[0]).results[0]["out"]
```
